# Optimizing a Trainium2 kernel written in Bass

```python
import jax, jax.numpy as jnp
from jax import lax
import numpy as np

D_MODEL = 1024
BATCH = 1
SEQ = 1024
DEPTH = 1
DEC_BATCH = 1
DEC_SEQ = 32
PAST_LEN = 1024

CHUNK = 64
Q_BLOCK = 128
EPS = 1e-6

GLA_HEADS = 4
GLA_DK = 64
GLA_DV = 128
GLA_LOWRANK = 16
GLA_GATE_NORM = 16.0

FOX_HEADS = 8
FOX_HD = 64
FOX_SCALE = FOX_HD ** -0.5

MIX_WIDTH = GLA_HEADS * GLA_DV + FOX_HEADS * FOX_HD

IN_SIZES = (GLA_HEADS * GLA_DK, GLA_HEADS * GLA_DK, GLA_HEADS * GLA_DV, GLA_HEADS * GLA_DV,
            GLA_LOWRANK, FOX_HEADS * FOX_HD, FOX_HEADS * FOX_HD, FOX_HEADS * FOX_HD, FOX_HEADS)
IN_WIDTH = sum(IN_SIZES)

PEER_HEADS = 8
PEER_NKEYS = 128
PEER_NEXP = PEER_NKEYS * PEER_NKEYS
PEER_DKEY = 256
PEER_TOPK = 16
PEER_BLOCK = 512

kernel_name = 'hybrid_gla_fox_peer_stream_step'

def _split_points():
    pts, acc = [], 0
    for s in IN_SIZES[:-1]:
        acc += s
        pts.append(acc)
    return pts

def rmsnorm(x, g):
    xf = x.astype(jnp.float32)
    y = xf * lax.rsqrt(jnp.mean(xf * xf, axis=-1, keepdims=True) + EPS)
    return (y * g.astype(jnp.float32)).astype(x.dtype)

def gla_recurrence(q, k, v, log_a, S0):
    B, T, H, Dk = q.shape
    Dv = v.shape[-1]
    L = min(T, CHUNK)
    n = T // L

    def to_chunks(a):
        return a.reshape(B, n, L, H, a.shape[-1]).transpose(1, 0, 3, 2, 4)

    qc = to_chunks(q.astype(jnp.float32) * (GLA_DK ** -0.5))
    kc = to_chunks(k.astype(jnp.float32))
    vc = to_chunks(v.astype(jnp.float32))
    ac = to_chunks(log_a)
    causal = jnp.tril(jnp.ones((L, L), dtype=bool))

    def step(S, inp):
        qb, kb, vb, ab = inp
        b = jnp.cumsum(ab, axis=2)
        b_last = b[:, :, -1, :]
        o_inter = jnp.einsum('bhld,bhdv->bhlv', qb * jnp.exp(b), S)
        diff = b[:, :, :, None, :] - b[:, :, None, :, :]
        decay = jnp.exp(jnp.where(causal[:, :, None], diff, -jnp.inf))
        A = jnp.einsum('bhtd,bhsd,bhtsd->bhts', qb, kb, decay)
        o = o_inter + jnp.einsum('bhts,bhsv->bhtv', A, vb)
        S_new = jnp.exp(b_last)[..., None] * S + jnp.einsum(
            'bhsd,bhsv->bhdv', kb * jnp.exp(b_last[:, :, None, :] - b), vb)
        return S_new, o

    S_fin, o = lax.scan(step, S0.astype(jnp.float32), (qc, kc, vc, ac))
    o = o.transpose(1, 0, 3, 2, 4).reshape(B, T, H, Dv)
    return o, S_fin

def fox_attention(q, k_all, v_all, c_all, P):
    B, T, H, D = q.shape
    S = k_all.shape[1]
    qb = min(T, Q_BLOCK)
    nb = T // qb
    cT = c_all.transpose(0, 2, 1)
    c_q = cT[:, :, P:]
    q_blocks = q.reshape(B, nb, qb, H, D).transpose(1, 0, 2, 3, 4)
    cq_blocks = c_q.reshape(B, H, nb, qb).transpose(2, 0, 1, 3)
    pos_blocks = (P + jnp.arange(T)).reshape(nb, qb)
    pos_k = jnp.arange(S)

    def block(inp):
        qi, ci, pi = inp
        s = jnp.einsum('bqhd,bkhd->bhqk', qi, k_all, preferred_element_type=jnp.float32) * FOX_SCALE
        s = s + ci[..., None] - cT[:, :, None, :]
        s = jnp.where(pos_k[None, :] <= pi[:, None], s, -jnp.inf)
        p = jax.nn.softmax(s, axis=-1)
        return jnp.einsum('bhqk,bkhd->bqhd', p.astype(v_all.dtype), v_all)

    out = lax.map(block, (q_blocks, cq_blocks, pos_blocks))
    return out.transpose(1, 0, 2, 3, 4).reshape(B, T, H, D)

def peer(h, w_q, subkeys, u_tab, v_tab):
    B, T, D = h.shape
    n = B * T
    blk = min(PEER_BLOCK, n)
    nb = -(-n // blk)
    pad = nb * blk - n
    xf = jnp.pad(h.reshape(n, D), ((0, pad), (0, 0))).reshape(nb, blk, D)

    def block(xb):
        q = (xb @ w_q).reshape(blk, PEER_HEADS, 2, PEER_DKEY // 2)
        s = jnp.einsum('nhcd,hckd->nhck', q, subkeys, preferred_element_type=jnp.float32)
        s1, i1 = lax.top_k(s[:, :, 0], PEER_TOPK)
        s2, i2 = lax.top_k(s[:, :, 1], PEER_TOPK)
        cand = (s1[..., :, None] + s2[..., None, :]).reshape(blk, PEER_HEADS, PEER_TOPK * PEER_TOPK)
        top, ti = lax.top_k(cand, PEER_TOPK)
        e1 = jnp.take_along_axis(i1, ti // PEER_TOPK, axis=-1)
        e2 = jnp.take_along_axis(i2, ti % PEER_TOPK, axis=-1)
        idx = e1 * PEER_NKEYS + e2
        g = jax.nn.softmax(top, axis=-1)
        u = jnp.take(u_tab, idx, axis=0)
        a = jax.nn.gelu(jnp.einsum('nhkd,nd->nhk', u, xb, preferred_element_type=jnp.float32),
                        approximate=False)
        coeff = (g * a).astype(v_tab.dtype)
        vsel = jnp.take(v_tab, idx, axis=0)
        return jnp.einsum('nhk,nhkd->nd', coeff, vsel)

    out = lax.map(block, xf).reshape(nb * blk, D)[:n]
    return out.reshape(B, T, D).astype(h.dtype)

def trunk_layer(x, S0, k_past, v_past, logf_past, g_norm1, w_in, w_gla_a2, b_gla_a, g_gla_onorm,
                g_fox_qnorm, g_fox_knorm, b_fox_f, w_out, g_norm2, w_peer_q, peer_subkeys,
                peer_u, peer_v):
    B, T, _ = x.shape
    P = k_past.shape[1]
    h = rmsnorm(x, g_norm1)
    z = h @ w_in
    gq, gk, gv, gg, glr, fq, fk, fv, ff = jnp.split(z, _split_points(), axis=-1)
    gq = gq.reshape(B, T, GLA_HEADS, GLA_DK)
    gk = gk.reshape(B, T, GLA_HEADS, GLA_DK)
    gv = gv.reshape(B, T, GLA_HEADS, GLA_DV)
    log_a = jax.nn.log_sigmoid((glr @ w_gla_a2 + b_gla_a).astype(jnp.float32)) / GLA_GATE_NORM
    log_a = log_a.reshape(B, T, GLA_HEADS, GLA_DK)
    o_gla, S_new = gla_recurrence(gq, gk, gv, log_a, S0)
    o_gla = rmsnorm(o_gla.astype(x.dtype), g_gla_onorm) * jax.nn.silu(gg.reshape(B, T, GLA_HEADS, GLA_DV))
    fq = rmsnorm(fq.reshape(B, T, FOX_HEADS, FOX_HD), g_fox_qnorm)
    fk = rmsnorm(fk.reshape(B, T, FOX_HEADS, FOX_HD), g_fox_knorm)
    fv = fv.reshape(B, T, FOX_HEADS, FOX_HD)
    logf = jax.nn.log_sigmoid((ff + b_fox_f).astype(jnp.float32))
    k_all = jnp.concatenate([k_past.astype(fk.dtype), fk], axis=1)
    v_all = jnp.concatenate([v_past.astype(fv.dtype), fv], axis=1)
    c_all = jnp.cumsum(jnp.concatenate([logf_past.astype(jnp.float32), logf], axis=1), axis=1)
    o_fox = fox_attention(fq, k_all, v_all, c_all, P)
    mixed = jnp.concatenate([o_gla.reshape(B, T, GLA_HEADS * GLA_DV),
                             o_fox.reshape(B, T, FOX_HEADS * FOX_HD).astype(x.dtype)], axis=-1) @ w_out
    x = x + mixed
    x = x + peer(rmsnorm(x, g_norm2), w_peer_q, peer_subkeys, peer_u, peer_v)
    return x, S_new, fk, fv, logf

def setup_inputs(seed: int = 0) -> dict:
    key = jax.random.key(seed)
    ks = jax.random.split(key, 20)
    f32 = jnp.float32

    def nrm(k, shape, scale):
        return scale * jax.random.normal(k, shape, f32)

    return dict(
        x_prompt=nrm(ks[0], (BATCH, SEQ, D_MODEL), 1.0),
        x_sample=nrm(ks[1], (DEC_BATCH, DEC_SEQ, D_MODEL), 1.0),
        cache_fox_k=nrm(ks[2], (DEPTH, DEC_BATCH, PAST_LEN, FOX_HEADS, FOX_HD), 1.0),
        cache_fox_v=nrm(ks[3], (DEPTH, DEC_BATCH, PAST_LEN, FOX_HEADS, FOX_HD), 1.0),
        cache_fox_logf=jax.nn.log_sigmoid(1.0 + jax.random.normal(ks[4], (DEPTH, DEC_BATCH, PAST_LEN, FOX_HEADS), f32)),
        state_gla=nrm(ks[5], (DEPTH, DEC_BATCH, GLA_HEADS, GLA_DK, GLA_DV), 0.5),
        g_norm1=1.0 + nrm(ks[6], (DEPTH, D_MODEL), 0.02),
        w_in=nrm(ks[7], (DEPTH, D_MODEL, IN_WIDTH), D_MODEL ** -0.5),
        w_gla_a2=nrm(ks[8], (DEPTH, GLA_LOWRANK, GLA_HEADS * GLA_DK), GLA_LOWRANK ** -0.5),
        b_gla_a=nrm(ks[9], (DEPTH, GLA_HEADS * GLA_DK), 0.1),
        g_gla_onorm=1.0 + nrm(ks[10], (DEPTH, GLA_DV), 0.02),
        g_fox_qnorm=1.0 + nrm(ks[11], (DEPTH, FOX_HD), 0.02),
        g_fox_knorm=1.0 + nrm(ks[12], (DEPTH, FOX_HD), 0.02),
        b_fox_f=1.0 + nrm(ks[13], (DEPTH, FOX_HEADS), 0.1),
        w_out=nrm(ks[14], (DEPTH, MIX_WIDTH, D_MODEL), MIX_WIDTH ** -0.5),
        g_norm2=1.0 + nrm(ks[15], (DEPTH, D_MODEL), 0.02),
        w_peer_q=nrm(ks[16], (DEPTH, D_MODEL, PEER_HEADS * PEER_DKEY), D_MODEL ** -0.5),
        peer_subkeys=nrm(ks[17], (DEPTH, PEER_HEADS, 2, PEER_NKEYS, PEER_DKEY // 2), (PEER_DKEY // 2) ** -0.5),
        peer_u=nrm(ks[18], (DEPTH, PEER_NEXP, D_MODEL), D_MODEL ** -0.5),
        peer_v=nrm(ks[19], (DEPTH, PEER_NEXP, D_MODEL), PEER_HEADS ** -0.5),
    )

def reference(x_prompt, x_sample, cache_fox_k, cache_fox_v, cache_fox_logf, state_gla,
              g_norm1, w_in, w_gla_a2, b_gla_a, g_gla_onorm, g_fox_qnorm, g_fox_knorm, b_fox_f,
              w_out, g_norm2, w_peer_q, peer_subkeys, peer_u, peer_v):
    yp, ys = x_prompt, x_sample
    Bp = x_prompt.shape[0]
    pk, pv, pf, pS = [], [], [], []
    sk, sv, sf, sS = [], [], [], []
    for l in range(DEPTH):
        params = (g_norm1[l], w_in[l], w_gla_a2[l], b_gla_a[l], g_gla_onorm[l], g_fox_qnorm[l],
                  g_fox_knorm[l], b_fox_f[l], w_out[l], g_norm2[l], w_peer_q[l], peer_subkeys[l],
                  peer_u[l], peer_v[l])
        S0 = jnp.zeros((Bp, GLA_HEADS, GLA_DK, GLA_DV), jnp.float32)
        k0 = jnp.zeros((Bp, 0, FOX_HEADS, FOX_HD), yp.dtype)
        f0 = jnp.zeros((Bp, 0, FOX_HEADS), jnp.float32)
        yp, S_p, k_p, v_p, f_p = trunk_layer(yp, S0, k0, k0, f0, *params)
        ys, S_s, k_s, v_s, f_s = trunk_layer(ys, state_gla[l], cache_fox_k[l], cache_fox_v[l],
                                             cache_fox_logf[l], *params)
        pk.append(k_p); pv.append(v_p); pf.append(f_p); pS.append(S_p)
        sk.append(k_s); sv.append(v_s); sf.append(f_s); sS.append(S_s)
    return (yp, ys, jnp.stack(pk), jnp.stack(pv), jnp.stack(pf), jnp.stack(pS),
            jnp.stack(sk), jnp.stack(sv), jnp.stack(sf), jnp.stack(sS))


_drawn_inputs = setup_inputs


def setup_inputs(seed=0):
    import zlib

    import numpy as np

    out = dict(_drawn_inputs(seed))
    spreads = {}
    factors = {'g_gla_onorm': 2.863, 'g_fox_qnorm': 4.296, 'g_fox_knorm': 3.125, 'g_norm2': 3.511}
    for name, (base, spread) in spreads.items():
        noise = np.random.default_rng([zlib.crc32(name.encode()), seed]).standard_normal(out[name].shape)
        drawn = base * np.exp(spread * noise) if base else spread * noise
        out[name] = __import__('jax').numpy.asarray(drawn.astype(out[name].dtype))
    for name, factor in factors.items():
        out[name] = (out[name] * factor).astype(out[name].dtype)
    return out
```

```python
from contextlib import ExitStack

import concourse.bass as bass
from concourse import mybir

F32 = mybir.dt.float32
BF16 = mybir.dt.bfloat16
U32 = mybir.dt.uint32
ALU = mybir.AluOpType
ACT = mybir.ActivationFunctionType
AX = mybir.AxisListType

P = 128
D = 1024
KD = D // P
T = 1024
TILES = T // P
ALL = TILES + 1
S_T = 32
COPIES = P // S_T
PAST = 1024
PB = PAST // P
EPS = 1e-6

GH, GK, GV, LR = 4, 64, 128, 16
FH, FD = 8, 64
GATE_NORM = 16.0
FOX_SCALE = FD ** -0.5
GLA_SCALE = GK ** -0.5

C_QK, C_GV, C_GG = 0, 2 * GH * GK, 2 * GH * GK + GH * GV
C_LR = C_GG + GH * GV
C_FQ = C_LR + LR
C_FK, C_FV = C_FQ + FH * FD, C_FQ + 2 * FH * FD
C_FF = C_FQ + 3 * FH * FD
WIN = C_FF + FH
GATES = GH * GK

PH, NKEY, DKEY, TOPK = 8, 128, 128, 16
SLOTS = PH * TOPK
LEVELS = [64, 32, 16, 8, 4, 2, 1]
NEG = -1.0e30
NEG_FILL = -3.0e38


def wait(eng, sem, count):
    if not isinstance(count, int) or count > 0:
        eng.wait_ge(sem, count)


def mix_phase(nc, ctx, io, dram, shared):
    def sb(n, s, d=F32):
        return ctx.enter_context(nc.sbuf_tensor(n, s, d))

    def ps(n, s, d=F32):
        return ctx.enter_context(nc.psum_tensor(n, s, d))

    w = sb("w_in", [P, KD, WIN])
    g1 = sb("g_norm1", [P, KD])
    ident = sb("ident", [P, P])
    tri = sb("tri", [P, 2, P])
    masks = sb("level_masks", [P, len(LEVELS) + 1, P], U32)
    wa = sb("w_gate", [LR, GATES])
    ba = sb("b_gate", [1, GATES])
    ones = sb("ones_row", [1, P])
    bf = sb("b_forget", [P, FH])
    gon = sb("g_out_norm", [P, GV])
    gqk = sb("g_qk_norm", [P, 2, FD])
    eps = sb("eps_mix", [P, 1])

    xT = [sb(f"x_T{b}", [P, KD, P]) for b in range(2)]
    xr = [sb(f"x_rows{b}", [P, D]) for b in range(2)]
    ss = sb("x_sumsq", [P, 1])
    std = sb("x_std", [P, 1])
    rstd = [sb(f"x_rstd{b}", [P, 1]) for b in range(2)]
    zqk = [sb(f"z_gla_qk{b}", [P, 512]) for b in range(2)]
    zv = [sb(f"z_gla_v{b}", [P, 512]) for b in range(2)]
    zg = [sb(f"z_gla_g{b}", [P, 512]) for b in range(2)]
    zs = [sb(f"z_small{b}", [P, LR + FH]) for b in range(2)]
    fqk = [sb(f"fox_qk{b}", [P, 2, 512]) for b in range(2)]
    fv = [sb(f"fox_v{b}", [P, 512]) for b in range(2)]
    lrT = sb("lowrank_T", [LR, P])
    gx = sb("gate_logits", [P, GATES + FH])
    ga = sb("gate_abs", [P, GATES + FH])
    ge = sb("gate_exp", [P, GATES + FH])
    gl = sb("gate_ln", [P, GATES + FH])
    ls = [sb(f"log_gates{b}", [P, GATES + FH]) for b in range(2)]
    nc_T = [sb(f"neg_c_T{b}", [FH, P]) for b in range(2)]
    carry = sb("neg_c_carry", [FH, 1])
    pastf = sb("past_logf", [P, PB * FH])
    past_sum = sb("past_block_sums", [PB * FH, 1])
    past_carry = sb("past_block_carry", [PB * FH, 1])
    past_nc = sb("past_neg_c", [PB * FH, P])
    earlier = sb("earlier_blocks", [PB * FH, PB * FH + FH])
    qT = sb("gla_q_T", [GK, GH, P])
    kT = sb("gla_k_T", [GK, GH, P])
    bT = sb("b_T", [GK, GH, P])
    eb = sb("exp_b", [GK, GH, P])
    ekd = sb("exp_last_minus_b", [GK, GH, P])
    qe = sb("q_exp_b", [GK, GH, P])
    kd = sb("k_decayed_T", [GK, GH, P])
    kdr = sb("k_decayed", [P, 2 * P])
    lev = sb("level_exp", [GK, len(LEVELS), GH, P])
    lq = [sb(f"level_q{b}", [GK, GH, P]) for b in range(2)]
    lk = [sb(f"level_k{b}", [GK, GH, P]) for b in range(2)]
    AT = sb("A_T", [P, GH, P])
    S = sb("gla_state", [GK, GH, GV])
    osq = sb("o_squared", [P, GH, GV])
    oss = sb("o_sumsq", [P, GH])
    ostd = sb("o_std", [P, GH])
    ors = sb("o_rstd", [P, GH])
    mixg = [sb(f"mix_gla{b}", [P, GH * GV]) for b in range(2)]
    fsq = sb("fox_squared", [P, 2, 512])
    fss = sb("fox_sumsq", [P, 2 * FH])
    fstd = sb("fox_std", [P, 2 * FH])
    frs = sb("fox_rstd", [P, 2 * FH])

    Z = [ps(f"ps_z{b}", [P, 512]) for b in range(2)]
    G = ps("ps_gate_ds", [P, 512])
    C = ps("ps_cumsum", [P, 512])
    TQ = ps("ps_q_T_level", [P, GH, P])
    TK = ps("ps_k_T", [P, GH, P])
    LP = [ps("ps_level", [P, GH, P]), TQ]
    O = ps("ps_o", [P, GH, GV])
    la_ps, cT_ps, lrT_ps = G[:, 0:GATES], G[0:FH, 256:384], G[0:LR, 384:512]
    bT_ps = ds_ps = C[0:GK, :].rearrange("p (h v) -> p h v", h=GH)
    kdr_ps = TK[:, 0:2, :].rearrange("p a t -> p (a t)")

    CH = [(C_LR, LR), (C_QK, 512), (C_GV, 512), (C_GG, 512), (C_FQ, 512), (C_FK, 512), (C_FV, 512)]
    NCH = len(CH)
    SMALL, QK, VV, GG, FQ, FK, FV = range(NCH)

    def sem(n):
        return ctx.enter_context(nc.semaphore(n))

    cst = sem("mix_consts_loaded")
    past_in = sem("past_logf_loaded")
    w_ld = [sem(f"w_in_loaded{k}") for k in range(KD)]
    w_sc = sem("w_in_scaled")
    inited = sem("mix_inited")
    x_in = [sem(f"x_loaded{b}") for b in range(2)]
    x_sq = sem("x_squared")
    x_std = sem("x_std_ready")
    x_rs = sem("x_rstd_ready")
    z_mm = sem("z_projected")
    z_ev = sem("z_in_sbuf")
    lr_t = sem("lowrank_transposed")
    lr_ev = sem("lowrank_T_ready")
    la_mm = sem("gate_projected")
    gx_r = sem("gate_logits_ready")
    g_abs = sem("gate_abs_ready")
    g_exp = sem("gate_exp_ready")
    g_ln = sem("gate_ln_ready")
    ls_r = sem("log_gates_ready")
    cum = sem("cumsums_done")
    b_r = sem("b_T_ready")
    c_r = sem("neg_c_ready")
    c_c = sem("neg_c_carried")
    past_mm = sem("past_cumsum_done")
    past_s = sem("past_sums_ready")
    past_c = sem("past_carry_done")
    past_r = sem("past_neg_c_ready")
    past_st = sem("past_neg_c_stored")
    qk_t = sem("gla_qk_transposed")
    qk_ev = sem("gla_qk_T_ready")
    eb_r = sem("exp_b_ready")
    qekd = sem("q_exp_b_k_decayed_ready")
    arg = sem("level_args_ready")
    lexp = sem("level_exps_ready")
    lqk = sem("level_qk_ready")
    lmm = sem("level_products_done")
    lsel = sem("level_selected")
    at0 = sem("A_T_cleared")
    kd_t = sem("k_decayed_transposed")
    kd_ev = sem("k_decayed_rows_ready")
    o_mm = sem("o_done")
    ds_mm = sem("state_step_done")
    s_up = sem("state_updated")
    s_ld = sem("sample_state_loaded")
    o_sq = sem("o_squares_done")
    o_std = sem("o_std_ready")
    o_rs = sem("o_rstd_ready")
    silu = sem("silu_ready")
    sg = sem("silu_g_ready")
    mixd = sem("mix_gla_ready")
    f_sq = sem("fox_squares_done")
    f_ss = sem("fox_sumsq_done")
    f_std = sem("fox_std_ready")
    f_rs = sem("fox_rstd_ready")
    f_n = sem("fox_scaled")
    f_g = sem("fox_normed")
    stored = sem("mix_stores_landed")
    flushed = sem("mix_tiles_flushed")
    s_st = sem("gla_states_landed")
    passed = sem("mix_waits_passed")

    LV = len(LEVELS)
    NL = LV + 1
    s_levels = [l for l, half in enumerate(LEVELS) if half < S_T]

    def levels(sample):
        return s_levels if sample else list(range(LV))

    def last(sample):
        return S_T if sample else P

    def over_tiles(eng, tile, prompt_done=None):
        for b in range(2):
            tile(b, b, 1, False)
        with eng.Fori(1, TILES // 2) as i:
            for b in range(2):
                tile(2 * i + b, b, i + 1, False)
        if prompt_done:
            prompt_done()
        tile(TILES, 0, TILES // 2 + 1, True)

    block = ctx.enter_context(nc.Block())

    @block.sync
    def _(sp):
        for dst, src in ((g1[:], dram["g1"]), (ident[:], dram["ident"]),
                         (tri[:], dram["tri"]), (masks[:], dram["masks"]), (wa[:], io["w_gla_a2"][0]),
                         (ba[:], io["b_gla_a"]), (bf[:], io["b_fox_f"].to_broadcast([P, FH])),
                         (gon[:], io["g_gla_onorm"].to_broadcast([P, GV])),
                         (gqk[:, 0, :], io["g_fox_qnorm"].to_broadcast([P, FD])),
                         (gqk[:, 1, :], io["g_fox_knorm"].to_broadcast([P, FD])),
                         (earlier[:], dram["earlier"])):
            sp.dma_start(dst, src).then_inc(cst, 16)
        for k in range(KD):
            sp.dma_start(w[:, k, :], io["w_in"][0, k * P:(k + 1) * P, :]).then_inc(w_ld[k], 16)
        sp.dma_start(pastf[:].rearrange("p (n h) -> p n h", h=FH),
                     io["cache_fox_logf"][0, 0].rearrange("(n p) h -> p n h", p=P)).then_inc(past_in, 16)

    @block.gpsimd
    def _(pool):
        def load(t, b):
            pool.dma_start(xT[b][:].rearrange("p k t -> p (k t)"), dram["xT"][bass.ds(t, 1)].rearrange("o p n -> (o p) n")).then_inc(x_in[b], 16)
            pool.dma_start(xr[b][:], dram["xr"][bass.ds(t, 1)].rearrange("o p n -> (o p) n")).then_inc(x_in[b], 16)

        def stores(t, b, u, sample):
            out = "s" if sample else "p"
            rows = last(sample)

            def at(name):
                return io[out + name] if sample else io[out + name][bass.ts(t, P), :]

            def scratch(name):
                return dram[name][bass.ds(t, 1)].rearrange("o p n -> (o p) n")
            if not sample:
                wait(pool, z_mm, t * NCH)
                wait(pool, x_sq, t)
                pool.sem_inc(passed, 1)
                load(t + 1, 1 - b)
            wait(pool, ls_r, t + 1)
            pool.sem_inc(passed, 1)
            pool.dma_start(at("_fox_logf"), ls[b][0:rows, GATES:GATES + FH]).then_inc(stored, 16)
            wait(pool, c_r, t + 1)
            pool.sem_inc(passed, 1)
            pool.dma_start(dram["negc"][:, bass.ts(t, P)], nc_T[b][:]).then_inc(stored, 16)
            wait(pool, z_ev, NCH * (t + 1))
            pool.sem_inc(passed, 1)
            pool.dma_start(at("_fox_v"), fv[b][0:rows, :]).then_inc(stored, 16)
            wait(pool, f_g, 2 * (t + 1))
            pool.sem_inc(passed, 1)
            pool.dma_start(at("_fox_k"), fqk[b][0:rows, 1, :]).then_inc(stored, 16)
            pool.dma_start(scratch("q"), fqk[b][:, 0, :]).then_inc(stored, 16)
            wait(pool, mixd, GH * (t + 1))
            pool.sem_inc(passed, 1)
            pool.dma_start(scratch("mixg"), mixg[b][:]).then_inc(stored, 16)
            wait(pool, stored, 96 * (t + 1))
            pool.sem_inc(flushed, 1)

        def swap_state():
            pool.wait_ge(s_up, GH * TILES)
            pool.dma_start(io["p_state"].rearrange("h k v -> k h v"), S[:]).then_inc(s_st, 16)
            pool.wait_ge(s_st, 16)
            pool.dma_start(S[:], io["state_gla"].rearrange("h k v -> k h v")).then_inc(s_ld, 16)
            pool.wait_ge(past_r, 1)
            pool.dma_start(dram["negc_past"], past_nc[:]).then_inc(past_st, 16)
        load(0, 0)
        over_tiles(pool, stores, swap_state)
        pool.wait_ge(s_up, GH * ALL)
        pool.dma_start(io["s_state"].rearrange("h k v -> k h v"), S[:]).then_inc(s_st, 16)
        pool.wait_ge(s_st, 32)
        pool.wait_ge(past_st, 16)

    @block.scalar
    def _(act):
        def tile(t, b, u, sample):
            n_last = last(sample)
            lv = levels(sample)
            wait(act, x_in[b], 32 * u)
            act.activation(xr[b][:], xr[b][:], ACT.Square, accum_out=ss[:]).then_inc(x_sq, 1)
            wait(act, x_sq, t + 1)
            act.activation(std[:], ss[:], ACT.Sqrt, bias=eps[:], scale=1.0 / D).then_inc(x_std, 1)
            wait(act, x_rs, t + 1)
            wait(act, flushed, t - 1)

            def evac(c, dst):
                wait(act, z_mm, t * NCH + c + 1)
                act.activation(dst, Z[c % 2][:, 0:dst.shape[-1]], ACT.Copy, scale=rstd[b][:]).then_inc(z_ev, 1)
            evac(SMALL, zs[b][:])
            evac(QK, zqk[b][:])
            wait(act, lr_t, t + 1)
            act.activation(lrT[:], lrT_ps, ACT.Copy).then_inc(lr_ev, 1)
            evac(VV, zv[b][:])
            wait(act, qk_t, t + 1)
            act.activation(qT[:], TQ[0:GK], ACT.Copy, scale=GLA_SCALE).then_inc(qk_ev, 1)
            act.activation(kT[:], TK[0:GK], ACT.Copy).then_inc(qk_ev, 1)
            wait(act, gx_r, 2 * (t + 1))
            act.activation(ga[:], gx[:], ACT.Abs).then_inc(g_abs, 1)
            wait(act, g_abs, t + 1)
            act.activation(ge[:], ga[:], ACT.Exp, scale=-1.0).then_inc(g_exp, 1)
            wait(act, g_exp, t + 1)
            act.activation(gl[:], ge[:], ACT.Ln, bias=1.0).then_inc(g_ln, 1)
            evac(GG, zg[b][:])
            evac(FQ, fqk[b][:, 0, :])
            wait(act, b_r, t + 1)
            wait(act, s_up, GH * t)
            act.activation(eb[:], bT[:], ACT.Exp).then_inc(eb_r, 1)
            for h in range(GH):
                act.activation(ekd[:, h, :], bT[:, h, :], ACT.Exp, bias=bT[:, h, n_last - 1:n_last], scale=-1.0).then_inc(eb_r, 1)
            evac(FK, fqk[b][:, 1, :])
            evac(FV, fv[b][:])
            wait(act, arg, 2 * LV * t + 2 * len(lv))
            act.activation(lev[:, lv[0]:, :, :], lev[:, lv[0]:, :, :], ACT.Exp).then_inc(lexp, 1)
            wait(act, z_ev, t * NCH + GG + 1)
            act.activation(zg[b][:], zg[b][:], ACT.Silu).then_inc(silu, 1)
            wait(act, f_ss, t + 1)
            act.activation(fstd[:], fss[:], ACT.Sqrt, bias=eps[:], scale=1.0 / FD).then_inc(f_std, 1)
            wait(act, kd_t, t + 1)
            act.activation(kdr[:], kdr_ps, ACT.Copy).then_inc(kd_ev, 1)
            wait(act, o_mm, t + 1)
            for h in range(GH):
                act.activation(osq[:, h, :], O[:, h, :], ACT.Square, accum_out=oss[:, h:h + 1]).then_inc(o_sq, 1)
            wait(act, o_sq, GH * (t + 1))
            act.activation(ostd[:], oss[:], ACT.Sqrt, bias=eps[:], scale=1.0 / GV).then_inc(o_std, 1)

        act.wait_ge(inited, 1)
        over_tiles(act, tile)

    @block.tensor
    def _(pe):
        def tile(t, b, u, sample):
            kind = 1 if sample else 0
            lv = levels(sample)

            def project(c):
                wait(pe, z_ev, t * NCH + c - (1 if c else 0))
                off, n = CH[c]
                for k in range(KD):
                    if t is not None and c == SMALL:
                        pe.matmul(Z[0][:, 0:LR], xT[b][:, k, :], w[:, k, C_LR:C_LR + LR], start=(k == 0), stop=False, skip_group_check=True)
                        m = pe.matmul(Z[0][:, LR:LR + FH], xT[b][:, k, :], w[:, k, C_FF:C_FF + FH], start=False, stop=(k == KD - 1), skip_group_check=True)
                    else:
                        m = pe.matmul(Z[c % 2][:, 0:n], xT[b][:, k, :], w[:, k, off:off + n], start=(k == 0), stop=(k == KD - 1))
                m.then_inc(z_mm, 1)
            wait(pe, x_in[b], 32 * u)
            project(SMALL)
            project(QK)
            wait(pe, z_ev, t * NCH + SMALL + 1)
            wait(pe, c_r, t)
            pe.transpose(lrT_ps, zs[b][:, 0:LR], ident[:]).then_inc(lr_t, 1)
            project(VV)
            wait(pe, lr_ev, t + 1)
            pe.matmul(la_ps, lrT[:], wa[:], start=True, stop=False)
            pe.matmul(la_ps, ones[:], ba[:], start=False, stop=True).then_inc(la_mm, 1)
            wait(pe, z_ev, t * NCH + QK + 1)
            wait(pe, kd_ev, t)
            wait(pe, lsel, NL * t)
            pe.sem_inc(passed, 1)
            for h in range(2 * GH):
                m = pe.transpose((TQ if h < GH else TK)[0:GK, h % GH, :], zqk[b][:, h * GK:(h + 1) * GK], ident[:])
            m.then_inc(qk_t, 1)
            project(GG)
            project(FQ)
            wait(pe, ls_r, t + 1)
            wait(pe, s_up, GH * t)
            for h in range(GH):
                pe.matmul(bT_ps[:, h, :], ls[b][:, h * GK:(h + 1) * GK], tri[:, kind, :], start=True, stop=True)
            pe.matmul(cT_ps, ls[b][:, GATES:GATES + FH], tri[:, kind, :], start=True, stop=True).then_inc(cum, 1)
            project(FK)
            project(FV)
            for n, l in enumerate([None] + lv):
                wait(pe, lsel, NL * t + n - 1)
                if n == 0:
                    wait(pe, qk_ev, 2 * (t + 1))
                    kk, qq = kT, qT
                else:
                    wait(pe, lqk, 2 * LV * t + 2 * n)
                    kk, qq = lk[n % 2], lq[n % 2]
                for h in range(GH):
                    m = pe.matmul(LP[n % 2][:, h, :], kk[:, h, :], qq[:, h, :], start=True, stop=True)
                m.then_inc(lmm, 1)
            wait(pe, qekd, 2 * (t + 1))
            wait(pe, qk_ev, 2 * (t + 1))
            pe.sem_inc(passed, 1)
            for h in range(GH):
                m = pe.transpose(kdr_ps[:, h * GK:(h + 1) * GK], kd[:, h, :], ident[0:GK, 0:GK])
            m.then_inc(kd_t, 1)
            wait(pe, lsel, NL * t + 1 + len(lv))
            wait(pe, mixd, GH * t)
            wait(pe, s_up, GH * t)
            wait(pe, z_ev, t * NCH + VV + 1)
            if sample:
                pe.wait_ge(s_ld, 16)
            for h in range(GH):
                pe.matmul(O[:, h, :], AT[:, h, :], zv[b][:, h * GV:(h + 1) * GV], start=True, stop=False)
                m = pe.matmul(O[:, h, :], qe[:, h, :], S[:, h, :], start=False, stop=True)
            m.then_inc(o_mm, 1)
            wait(pe, kd_ev, t + 1)
            n = last(sample)
            for h in range(GH):
                m = pe.matmul(ds_ps[:, h, :], kdr[0:n, h * GK:(h + 1) * GK], zv[b][0:n, h * GV:(h + 1) * GV], start=True, stop=True)
            m.then_inc(ds_mm, 1)

        def past():
            pe.wait_ge(past_in, 16)
            pe.wait_ge(s_up, GH * TILES)
            pe.matmul(C[0:PB * FH, 0:P], pastf[:], tri[:, 0, :], start=True, stop=True).then_inc(past_mm, 1)
            pe.wait_ge(past_s, 1)
            pe.matmul(C[0:PB * FH, 128:129], earlier[:, 0:PB * FH], past_sum[:], start=True, stop=True, skip_group_check=True)
            pe.matmul(C[0:FH, 256:257], earlier[:, PB * FH:], past_sum[:], start=True, stop=True, skip_group_check=True).then_inc(past_c, 1)
            pe.wait_ge(past_r, 2)
        pe.wait_ge(cst, 16 * 11)
        pe.wait_ge(w_sc, KD)
        over_tiles(pe, tile, past)

    @block.vector
    def _(dve):
        def tile(t, b, u, sample):
            n_last = last(sample)
            lv = levels(sample)
            wait(dve, x_std, t + 1)
            dve.reciprocal(rstd[b][:], std[:]).then_inc(x_rs, 1)
            wait(dve, flushed, t - 1)
            wait(dve, z_ev, t * NCH + SMALL + 1)
            wait(dve, ls_r, t)
            dve.tensor_tensor(gx[:, GATES:], zs[b][:, LR:], bf[:], ALU.add).then_inc(gx_r, 1)
            wait(dve, la_mm, t + 1)
            dve.tensor_copy(gx[:, 0:GATES], la_ps).then_inc(gx_r, 1)
            wait(dve, o_mm, t)
            dve.memset(AT[:], 0.0).then_inc(at0, 1)
            wait(dve, g_ln, t + 1)
            dve.scalar_tensor_tensor(out=ls[b][:], in0=gx[:], scalar=0.0, in1=gl[:], op0=ALU.min, op1=ALU.subtract).then_inc(ls_r, 1)
            wait(dve, cum, t + 1)
            wait(dve, c_c, t + 1)
            dve.tensor_scalar(nc_T[b][:], cT_ps, -1.0, carry[:], ALU.mult, ALU.add).then_inc(c_r, 1)
            wait(dve, c_r, t + 1)
            dve.tensor_copy(carry[:], nc_T[b][:, n_last - 1:n_last]).then_inc(c_c, 1)
            wait(dve, eb_r, 5 * t)
            dve.tensor_scalar(bT[:], bT_ps, 1.0 / GATE_NORM, None, ALU.mult).then_inc(b_r, 1)
            wait(dve, b_r, t + 1)
            for l in lv:
                half = LEVELS[l]
                bb = bT[:].rearrange("p i (n a x) -> p (i n) a x", a=2, x=half)
                mid = bb[:, :, 0, half - 1:half].to_broadcast([GK, bb.shape[1], half])
                ll = lev[:, l, :, :].rearrange("p i (n a x) -> p (i n) a x", a=2, x=half)
                wait(dve, lqk, 2 * LV * t)
                dve.tensor_tensor(ll[:, :, 1, :], bb[:, :, 1, :], mid, ALU.subtract).then_inc(arg, 1)
                dve.tensor_tensor(ll[:, :, 0, :], mid, bb[:, :, 0, :], ALU.subtract).then_inc(arg, 1)
            wait(dve, eb_r, 5 * (t + 1))
            wait(dve, qk_ev, 2 * (t + 1))
            wait(dve, kd_t, t)
            dve.tensor_tensor(qe[:], qT[:], eb[:], ALU.mult).then_inc(qekd, 1)
            dve.tensor_tensor(kd[:], kT[:], ekd[:], ALU.mult).then_inc(qekd, 1)
            wait(dve, lexp, t + 1)
            wait(dve, at0, t + 1)

            def select(n, l):
                wait(dve, lmm, NL * t + n + 1)
                wait(dve, lsel, NL * t + n)
                dve.sem_inc(passed, 1)
                dve.copy_predicated(AT[:], masks[:, l, :].unsqueeze(1).to_broadcast([P, GH, P]), LP[n % 2][:]).then_inc(lsel, 1)
            for n, l in enumerate(lv):
                half = LEVELS[l]

                def view(x, a):
                    return x.rearrange("p i (n a x) -> p (i n) a x", a=2, x=half)[:, :, a, :]
                wait(dve, lmm, NL * t + n)
                o = (n + 1) % 2
                wait(dve, lqk, 2 * LV * t + 2 * n)
                dve.tensor_tensor(view(lq[o][:], 1), view(qT[:], 1), view(lev[:, l, :, :], 1), ALU.mult).then_inc(lqk, 1)
                dve.tensor_tensor(view(lk[o][:], 0), view(kT[:], 0), view(lev[:, l, :, :], 0), ALU.mult).then_inc(lqk, 1)
                select(n, lv[n - 1] if n else LV)
            select(len(lv), lv[-1])
            wait(dve, silu, t + 1)
            dve.tensor_tensor(zg[b][:].rearrange("p (h v) -> p h v", h=GH), zg[b][:].rearrange("p (h v) -> p h v", h=GH),
                              gon[:].unsqueeze(1).to_broadcast([P, GH, GV]), ALU.mult).then_inc(sg, 1)
            wait(dve, z_ev, t * NCH + FK + 1)
            wait(dve, f_ss, t)
            dve.tensor_tensor(fsq[:], fqk[b][:], fqk[b][:], ALU.mult).then_inc(f_sq, 1)
            wait(dve, f_sq, t + 1)
            dve.tensor_reduce(fss[:], fsq[:].rearrange("p c (h d) -> p (c h) d", d=FD), AX.X, ALU.add).then_inc(f_ss, 1)
            wait(dve, f_std, t + 1)
            dve.reciprocal(frs[:], fstd[:]).then_inc(f_rs, 1)
            wait(dve, f_rs, t + 1)
            rows = fqk[b][:].rearrange("p c (h d) -> p (c h) d", d=FD)
            dve.tensor_tensor(rows, rows, frs[:].unsqueeze(2).to_broadcast([P, 2 * FH, FD]), ALU.mult).then_inc(f_n, 1)
            wait(dve, f_n, t + 1)
            for c in range(2):
                rows = fqk[b][:, c, :].rearrange("p (h d) -> p h d", d=FD)
                dve.tensor_tensor(rows, rows, gqk[:, c, :].unsqueeze(1).to_broadcast([P, FH, FD]), ALU.mult).then_inc(f_g, 1)
            wait(dve, ds_mm, t + 1)
            for h in range(GH):
                dve.scalar_tensor_tensor(out=S[:, h, :], in0=S[:, h, :], scalar=eb[:, h, n_last - 1:n_last], in1=ds_ps[:, h, :],
                                         op0=ALU.mult, op1=ALU.add).then_inc(s_up, 1)
            wait(dve, o_std, t + 1)
            dve.reciprocal(ors[:], ostd[:]).then_inc(o_rs, 1)
            wait(dve, o_rs, t + 1)
            wait(dve, sg, t + 1)
            for h in range(GH):
                dve.scalar_tensor_tensor(out=mixg[b][:, h * GV:(h + 1) * GV], in0=O[:, h, :], scalar=ors[:, h:h + 1],
                                         in1=zg[b][:, h * GV:(h + 1) * GV], op0=ALU.mult, op1=ALU.mult).then_inc(mixd, 1)

        def past():
            dve.wait_ge(past_mm, 1)
            dve.tensor_copy(past_sum[:], C[0:PB * FH, P - 1:P]).then_inc(past_s, 1)
            dve.wait_ge(past_c, 1)
            dve.tensor_copy(past_carry[:], C[0:PB * FH, 128:129]).then_inc(past_s, 1)
            dve.wait_ge(past_s, 2)
            dve.tensor_scalar(past_nc[:], C[0:PB * FH, 0:P], past_carry[:], -1.0, ALU.add, ALU.mult).then_inc(past_r, 1)
            dve.wait_ge(c_c, TILES + 1)
            dve.tensor_scalar(carry[:], C[0:FH, 256:257], -1.0, None, ALU.mult).then_inc(past_r, 1)
            dve.wait_ge(past_r, 2)
            dve.wait_ge(s_ld, 16)
        dve.memset(eps[:], EPS).then_inc(inited, 1)
        dve.memset(ones[:], 1.0)
        dve.memset(carry[:], 0.0).then_inc(c_c, 1)
        dve.memset(S[:], 0.0)
        for b in range(2):
            dve.memset(lq[b][:], 0.0)
            dve.memset(lk[b][:], 0.0)
        dve.memset(lev[:], 0.0).then_inc(inited, 1)
        dve.wait_ge(cst, 16 * 11)
        for k in range(KD):
            dve.wait_ge(w_ld[k], 16)
            dve.tensor_scalar(w[:, k, :], w[:, k, :], g1[:, k:k + 1], None, ALU.mult).then_inc(w_sc, 1)
        over_tiles(dve, tile, past)


def attend_phase(nc, ctx, io, dram):
    def sb(n, s, d=F32):
        return ctx.enter_context(nc.sbuf_tensor(n, s, d))

    def ps(n, s, d=F32):
        return ctx.enter_context(nc.psum_tensor(n, s, d))

    def sem(n):
        return ctx.enter_context(nc.semaphore(n))

    KA = FD + 1
    w = sb("w_out", [P, KD, D])
    ident = sb("ident_f", [P, P])
    identb = sb("ident_b", [P, P], BF16)
    causal = sb("causal_neg", [P, 2, P], BF16)
    kT = sb("k_aug_T", [KA, FH, PAST + S_T])
    qT = sb("q_aug_T", [KA, FH, P])
    qh = [sb(f"q_head{b}", [KA, P]) for b in range(2)]
    v = sb("v_rows", [P, TILES + 1, FH * FD])
    kr = sb("k_rows", [P, FH * FD])
    qr = sb("q_rows", [P, FH * FD])
    xr = sb("x_res", [P, D])
    mix = sb("mix_rows", [P, D])
    mixT = sb("mix_T", [P, KD, P])
    xm = [sb(f"x_mid{b}", [P, D]) for b in range(2)]
    m = [sb(f"row_max{b}", [P, 1]) for b in range(2)]
    nm = [sb(f"neg_max{b}", [P, 1]) for b in range(2)]
    pr = [sb(f"prob_rows{b}", [P, PAST + S_T]) for b in range(2)]
    pT = [sb(f"prob_T{b}", [P, 4, P]) for b in range(2)]
    l = sb("row_sums", [P, FH])
    rl = sb("row_sums_inv", [P, FH])

    S = [ps("ps_scores0", [P, 1536]), ps("ps_scores1", [P, 1024])]
    Q = [ps(f"ps_quad{b}", [P, 4, P]) for b in range(2)]
    O = ps("ps_fox_o", [P, FH, FD])

    cst = sem("attend_consts_loaded")
    wld = sem("w_out_loaded")
    kv_in = sem("keys_values_loaded")
    t_in = sem("attend_rows_loaded")
    one = sem("aug_ones_set")
    kq_t = sem("kq_quads_transposed")
    kq_ev = sem("kq_quads_ready")
    q_cp = sem("q_head_copied")
    s_mm = sem("scores_done")
    mx = sem("row_max_ready")
    nmx = sem("neg_max_ready")
    ex = sem("probs_ready")
    p_t = sem("prob_quads_transposed")
    p_ev = sem("prob_quads_ready")
    pv = sem("prob_quads_used")
    rls = sem("row_sums_inverted")
    o_n = sem("fox_out_ready")
    mx_t = sem("mix_quads_transposed")
    mx_ev = sem("mix_T_ready")
    y_mm = sem("mixed_projected")
    xm_r = sem("x_mid_ready")
    xm_st = sem("x_mid_landed")
    passed = sem("attend_waits_passed")

    CR = 2

    def shape(t):
        blocks = [P] * (t + 1) if t < TILES else [P] * PB + [S_T]
        total = sum(blocks)
        chunks = [(a, min(a + 512, total)) for a in range(0, total, 512)]
        return blocks, total, chunks

    def quads(t):
        return -(-len(shape(t)[0]) // 4)

    def quads_before(t):
        return sum(FH * quads(u) for u in range(t))

    block = ctx.enter_context(nc.Block())

    @block.sync
    def _(sp):
        sp.dma_start(ident[:], dram["ident"]).then_inc(cst, 16)
        sp.dma_start(identb[:], dram["ident_b"]).then_inc(cst, 16)
        sp.dma_start(causal[:], dram["causal"]).then_inc(cst, 16)
        sp.dma_start(kT[FD:KA, :, 0:T], dram["negc"][:, 0:T].rearrange("(o h) t -> o h t", o=1)).then_inc(kv_in, 16)
        sp.dma_start(v[:, 0:TILES, :], io["p_fox_v"].rearrange("(n p) c -> p n c", p=P)).then_inc(kv_in, 16)
        for t in range(ALL):
            sample = t == TILES
            rows = S_T if sample else P
            if t:
                sp.wait_ge(kq_t, 4 * t)
                sp.wait_ge(o_n, t)
                sp.wait_ge(mx_t, 2 * t)
                sp.wait_ge(xm_r, 2 * t)
            if sample:
                sp.wait_ge(pv, quads_before(TILES) + CR)
                sp.dma_start(kT[0:FD, :, 0:PAST], dram["kT_past"]).then_inc(kv_in, 16)
                for h in range(FH):
                    sp.dma_start(kT[FD:KA, h, 0:PAST].rearrange("o (n t) -> o n t", t=P),
                                 dram["negc_past"][h:PB * FH:FH, :].rearrange("(o n) t -> o n t", o=1)).then_inc(kv_in, 16)
                sp.dma_start(kT[FD:KA, :, PAST:PAST + S_T], dram["negc"][:, T:T + S_T].rearrange("(o h) t -> o h t", o=1)).then_inc(kv_in, 16)
                sp.dma_start(v[:, 0:PB, :], io["cache_fox_v"].rearrange("(n p) c -> p n c", p=P)).then_inc(kv_in, 16)
                sp.dma_start(v[0:S_T, PB, :], io["s_fox_v"]).then_inc(kv_in, 16)
            k_src = io["s_fox_k"] if sample else io["p_fox_k"][t * P:(t + 1) * P, :]
            sp.dma_start(kr[0:rows, :], k_src).then_inc(t_in, 16)
            sp.dma_start(qr[:], dram["q"][t]).then_inc(t_in, 16)
            sp.dma_start(mix[:, 0:GH * GV], dram["mixg"][t]).then_inc(t_in, 16)
            sp.dma_start(xr[:], dram["xr"][t]).then_inc(t_in, 16)
            if t == 0:
                sp.dma_start(w[:], io["w_out"][0].rearrange("(k p) n -> p k n", p=P)).then_inc(wld, 16)
            if t:
                sp.dma_start(dram["xm"][t - 1], xm[(t - 1) % 2][:]).then_inc(xm_st, 16)
        sp.wait_ge(xm_r, 2 * ALL)
        sp.dma_start(dram["xm"][ALL - 1], xm[(ALL - 1) % 2][:]).then_inc(xm_st, 16)
        sp.wait_ge(xm_st, 16 * ALL)

    @block.gpsimd
    def _(pool):
        pool.sem_inc(q_cp, CR)
        pool.wait_ge(one, 1)
        for t in range(ALL):
            pool.wait_ge(kq_ev, 4 * (t + 1))
            with pool.Fori(0, FH // 2) as hp:
                for b in range(2):
                    g = FH * t + 2 * hp + b
                    pool.wait_ge(s_mm, g - 1 + CR)
                    pool.sem_inc(passed, 1)
                    pool.tensor_copy(qh[b][:], qT[:, bass.ds(2 * hp + b, 1), :].rearrange("k o t -> k (o t)")).then_inc(q_cp, 1)

    @block.scalar
    def _(act):
        act.sem_inc(ex, CR)
        for t in range(ALL):
            rows = S_T if t == TILES else P
            at = PAST if t == TILES else t * P
            for n in range(4):
                act.wait_ge(kq_t, 4 * t + n + 1)
                hs = slice(4 * (n % 2), 4 * (n % 2) + 4)
                if n < 2:
                    act.activation(kT[0:FD, hs, at:at + rows], Q[n % 2][0:FD, :, 0:rows], ACT.Copy).then_inc(kq_ev, 1)
                else:
                    act.wait_ge(q_cp, FH * t + CR)
                    act.activation(qT[0:FD, hs, :], Q[n % 2][0:FD], ACT.Copy, scale=FOX_SCALE).then_inc(kq_ev, 1)
            total = shape(t)[1]
            wait(act, o_n, t)
            with act.Fori(0, FH // 2) as hp:
                for b in range(2):
                    g = FH * t + 2 * hp + b
                    act.wait_ge(nmx, g + 1)
                    act.wait_ge(p_t, quads_before(t) + (2 * hp + b - 1) * quads(t) + CR)
                    act.sem_inc(passed, 1)
                    src = S[0 if t == TILES else b]
                    act.activation(pr[b][:, 0:total], src[:, 0:total], ACT.Exp, bias=nm[b][:],
                                   accum_out=l[:, bass.ds(2 * hp + b, 1)]).then_inc(ex, 1)
            for n in range(2):
                act.wait_ge(mx_t, 2 * t + n + 1)
                wait(act, y_mm, 2 * t)
                act.activation(mixT[:, 4 * n:4 * n + 4, :], Q[n][:], ACT.Copy).then_inc(mx_ev, 1)

    @block.tensor
    def _(pe):
        pe.sem_inc(s_mm, CR)
        pe.sem_inc(p_t, CR)
        pe.sem_inc(pv, CR)
        pe.wait_ge(cst, 48)
        for t in range(ALL):
            sample = t == TILES
            rows = S_T if sample else P
            blocks, total, chunks = shape(t)
            nq = quads(t)
            q0 = quads_before(t)
            pe.wait_ge(t_in, 64 * (t + 1))
            pe.wait_ge(p_ev, q0 + CR)
            wait(pe, mx_ev, 2 * t)
            for n in range(4):
                if n >= 2:
                    pe.wait_ge(kq_ev, 4 * t + n - 1)
                src, r = (kr, rows) if n < 2 else (qr, P)
                for h in range(4):
                    c = (4 * (n % 2) + h) * FD
                    tr = pe.transpose(Q[n % 2][0:FD, h, 0:r], src[0:r, c:c + FD], ident[0:r, 0:r])
                tr.then_inc(kq_t, 1)
            pe.wait_ge(kq_ev, 4 * (t + 1))
            pe.wait_ge(kv_in, 32 if not sample else 32 + 16 * (FH + 4))
            pe.wait_ge(one, 1)
            wait(pe, xm_r, 2 * t)

            def scores(h, g, b):
                pe.wait_ge(q_cp, g + 1 + CR)
                dst = S[0 if sample else b]
                pe.wait_ge(ex, g - (0 if sample else 1) + CR)
                pe.sem_inc(passed, 1)
                for lo, hi in chunks:
                    own = hi == total
                    mm = pe.matmul(dst[:, lo:hi], qh[b][:], kT[:, bass.ds(h, 1), lo:hi].rearrange("k o t -> k (o t)"), start=True, stop=not own)
                wd = blocks[-1]
                mm = pe.matmul(dst[:, total - wd:total], identb[:], causal[:, 1 if sample else 0, 0:wd], start=False, stop=True)
                mm.then_inc(s_mm, 1)

            def values(h, g, b, qh0):
                pe.wait_ge(ex, g + 1 + CR)
                pe.sem_inc(passed, 1)

                def turn(q):
                    e = (b * nq + q) % 2
                    pe.wait_ge(p_ev, q0 + qh0 + q - 1 + CR)
                    pe.sem_inc(passed, 1)
                    for n in range(4 * q, min(4 * q + 4, len(blocks))):
                        tr = pe.transpose(Q[e][0:blocks[n], n - 4 * q, :], pr[b][:, n * P:n * P + blocks[n]], ident[:])
                    tr.then_inc(p_t, 1)

                def use(q):
                    e = (b * nq + q) % 2
                    pe.wait_ge(p_ev, q0 + qh0 + q + 1 + CR)
                    pe.sem_inc(passed, 1)
                    for n in range(4 * q, min(4 * q + 4, len(blocks))):
                        mm = pe.matmul(O[:, bass.ds(h, 1), :].rearrange("p o d -> p (o d)"), pT[e][0:blocks[n], n - 4 * q, :],
                                       v[0:blocks[n], n, bass.ts(h, FD)], start=(n == 0), stop=(n == len(blocks) - 1))
                    mm.then_inc(pv, 1)
                turn(0)
                for q in range(nq):
                    if q + 1 < nq:
                        turn(q + 1)
                    use(q)

            wait(pe, o_n, t)
            with pe.Fori(0, FH // 2) as hp:
                for b in range(2):
                    g = FH * t + 2 * hp + b
                    scores(2 * hp + b, g, b)
                    values(2 * hp + b, g, b, (2 * hp + b) * nq)
            pe.wait_ge(o_n, t + 1)
            pe.wait_ge(p_ev, quads_before(t + 1) + CR)
            for n in range(2):
                for k in range(4):
                    tr = pe.transpose(Q[n][:, k, :], mix[:, (4 * n + k) * P:(4 * n + k + 1) * P], ident[:])
                tr.then_inc(mx_t, 1)
            pe.wait_ge(mx_ev, 2 * t + 2)
            pe.wait_ge(wld, 16)
            pe.wait_ge(ex, FH * (t + 1) + CR)
            for n in range(2):
                for k in range(KD):
                    mm = pe.matmul(S[1][:, n * 512:(n + 1) * 512], mixT[:, k, :], w[:, k, n * 512:(n + 1) * 512], start=(k == 0), stop=(k == KD - 1))
                mm.then_inc(y_mm, 1)

    @block.vector
    def _(dve):
        dve.memset(qT[FD:KA, :, :], 1.0).then_inc(one, 1)
        dve.sem_inc(p_ev, CR)
        for t in range(ALL):
            total = shape(t)[1]
            blocks = shape(t)[0]
            nq = quads(t)
            with dve.Fori(0, FH // 2) as hp:
                for b in range(2):
                    g = FH * t + 2 * hp + b
                    dve.wait_ge(s_mm, g + 1 + CR)
                    dve.tensor_reduce(m[b][:], S[0 if t == TILES else b][:, 0:total], AX.X, ALU.max).then_inc(mx, 1)
                    dve.wait_ge(mx, g + 1)
                    dve.wait_ge(ex, g - 1 + CR)
                    dve.tensor_scalar(nm[b][:], m[b][:], -1.0, None, ALU.mult).then_inc(nmx, 1)
                    for q in range(nq):
                        e = (b * nq + q) % 2
                        n = quads_before(t) + (2 * hp + b) * nq + q
                        dve.wait_ge(p_t, n + 1 + CR)
                        dve.wait_ge(pv, n - 1 + CR)
                        full = [x for x in blocks[4 * q:4 * q + 4] if x == P]
                        if full:
                            dve.tensor_copy(pT[e][:, 0:len(full), :], Q[e][:, 0:len(full), :]).then_inc(p_ev, 1)
                        else:
                            dve.tensor_copy(pT[e][0:S_T, 0, :], Q[e][0:S_T, 0, :]).then_inc(p_ev, 1)
            dve.wait_ge(ex, FH * (t + 1) + CR)
            dve.reciprocal(rl[:], l[:]).then_inc(rls, 1)
            dve.wait_ge(rls, t + 1)
            dve.wait_ge(pv, quads_before(t + 1) + CR)
            dve.wait_ge(t_in, 64 * (t + 1))
            dve.tensor_tensor(mix[:, GH * GV:].rearrange("p (h d) -> p h d", d=FD), O[:],
                              rl[:].unsqueeze(2).to_broadcast([P, FH, FD]), ALU.mult).then_inc(o_n, 1)
            for n in range(2):
                dve.wait_ge(y_mm, 2 * t + n + 1 if n else 2 * t + 2)
                wait(dve, xm_st, 16 * (t - 1))
                dve.tensor_tensor(xm[t % 2][:, n * 512:(n + 1) * 512], S[1][:, n * 512:(n + 1) * 512], xr[:, n * 512:(n + 1) * 512], ALU.add).then_inc(xm_r, 1)


def peer_phase(nc, ctx, io, dram):
    def sb(n, s, d=F32):
        return ctx.enter_context(nc.sbuf_tensor(n, s, d))

    def ps(n, s, d=F32):
        return ctx.enter_context(nc.psum_tensor(n, s, d))

    def sem(n):
        return ctx.enter_context(nc.semaphore(n))

    RING = 8
    STEP = 2 * RING
    GRP = 4
    K2 = TOPK * TOPK
    w = sb("w_peer_q", [P, KD, PH * 2 * DKEY])
    sub = sb("subkeys_T", [P, PH * 2, NKEY])
    g2 = sb("g_norm2_rows", [P, D])
    ident = sb("ident_p", [P, P])
    fold = sb("fold_copies", [P, P])
    iota = sb("iota16", [P, TOPK])
    eps = sb("eps_peer", [P, 1])
    xm = [sb(f"x_mid_in{b}", [P, D]) for b in range(2)]
    h2 = [sb(f"h2_rows{b}", [P, D]) for b in range(2)]
    h2T = sb("h2_T", [P, KD, P])
    hss = sb("h2_sumsq", [P, 1])
    hstd = sb("h2_std", [P, 1])
    hrs = sb("h2_rstd", [P, 1])
    qr = sb("peer_q_rows", [P, 2 * DKEY])
    qT = sb("peer_q_T", [P, 2, P])
    s1 = sb("key_scores", [P, 2, NKEY])
    s2 = sb("key_scores_rest", [P, 2, NKEY])
    kv = sb("key_top", [P, 2, TOPK])
    ki = sb("key_top_index", [P, 2, TOPK], U32)
    kf = sb("key_top_index_f", [P, 2, TOPK])
    cand = sb("candidates", [P, TOPK, TOPK])
    cand2 = sb("candidates_rest", [P, TOPK, TOPK])
    tv = sb("expert_top", [P, TOPK])
    ti = sb("expert_top_index", [P, TOPK], U32)
    ab = sb("expert_pair", [P, 2, TOPK], U32)
    abf = sb("expert_pair_f", [P, 2, TOPK])
    hot = sb("expert_pair_one_hot", [P, 2, TOPK, TOPK])
    pick = sb("expert_pair_keys", [P, 2, TOPK])
    nmx = sb("neg_top", [P, 1])
    pe_ = sb("top_exp", [P, TOPK])
    psum_ = sb("top_exp_sum", [P, 1])
    pinv = sb("top_exp_sum_inv", [P, 1])
    idx = [sb(f"expert_index{b}", [P, SLOTS], U32) for b in range(2)]
    gw = [sb(f"expert_weight{b}", [P, SLOTS]) for b in range(2)]
    idx_s = sb("sample_index", [P, SLOTS // COPIES], U32)
    gw_s = sb("sample_weight", [P, SLOTS // COPIES])
    ixs = sb("staged_index", [P, 2, RING], U32)
    ring = sb("uv_ring", [P, RING, 2 * D])
    dots = sb("u_dot_h", [P, 2, GRP])
    gel = sb("gelu_u_dot_h", [P, 2, GRP])
    coef = sb("coefficients", [P, 2, GRP])
    diag = sb("coef_diag", [P, RING, P])
    res = sb("y_rows", [P, D])

    acc = [ps(f"ps_acc{b}", [P, 2, 512]) for b in range(2)]
    TB = [ps(f"ps_turn{b}", [P, 4, P]) for b in range(2)]
    QR = ps("ps_q_rows", [P, 512])
    SC = ps("ps_key_scores", [P, 512])

    cst = sem("peer_consts_loaded")
    wld = sem("peer_weights_loaded")
    init = sem("peer_inited")
    x_in = [sem(f"x_mid_loaded{b}") for b in range(2)]
    p_sq = sem("h2_squared")
    p_std = sem("h2_std_ready")
    p_rs = sem("h2_rstd_ready")
    p_h2 = sem("h2_ready")
    p_t = sem("h2_transposed")
    p_ev = sem("h2_T_ready")
    q_mm = sem("peer_q_done")
    q_ev = sem("peer_q_rows_ready")
    qt_t = sem("peer_q_transposed")
    qt_ev = sem("peer_q_T_ready")
    s_mm = sem("key_scores_done")
    s_ev = sem("key_scores_ready")
    chain = sem("routing_steps")
    ex = sem("top_exp_ready")
    nmr = sem("neg_top_ready")
    routed = sem("head_routed")
    spread = sem("sample_slots_spread")
    staged = sem("index_staged")
    slot = [sem(f"uv_landed{r}") for r in range(RING)]
    dotted = sem("u_dotted")
    geld = sem("gelu_ready")
    cfd = sem("coefficients_ready")
    dgd = sem("diagonal_ready")
    summed = sem("v_summed")
    a_in = sem("acc_started")
    a_ev = sem("y_rows_ready")
    y_st = sem("y_landed")
    passed = sem("peer_waits_passed")
    CR = 2

    block = ctx.enter_context(nc.Block())

    def pipeline(eng, pre, step, last, finish):
        pre(0, 0, 1)
        with eng.Fori(0, PH) as j:
            step(None, 0, 0, 0, j)
        with eng.Fori(0, TILES // 2) as i:
            for b in range(2):
                t = 2 * i + b
                pre(t + 1, 1 - b, i + 1 + b)
                with eng.Fori(0, PH) as j:
                    step(t, b, t + 1, 1 - b, j)
                finish(t, b)
        last()
        with eng.Fori(0, PH // COPIES) as j:
            step(TILES, 0, None, 0, j)
        finish(TILES, 0)

    def nothing(*_):
        pass

    @block.sync
    def _(sp):
        for dst, src in ((ident[:], dram["ident"]), (fold[:], dram["fold"]), (iota[:], dram["iota"]),
                         (g2[:], io["g_norm2"].to_broadcast([P, D])), (sub[:], dram["subkeys_T"])):
            sp.dma_start(dst, src).then_inc(cst, 16)
        sp.dma_start(w[:], io["w_peer_q"][0].rearrange("(k p) n -> p k n", p=P)).then_inc(wld, 16)

    @block.gpsimd
    def _(pool):
        def step(t, b, rt, rb, j):
            if t is None:
                return
            base = SLOTS * t + STEP * j
            src = idx_s if rt is None else idx[b]
            for c in range(2):
                pool.wait_ge(summed, base + RING * c + 1)
                if rt is None:
                    pool.wait_ge(spread, 2 * COPIES)
                else:
                    pool.wait_ge(routed, PH * (t + 1) + CR)
                pool.sem_inc(passed, 1)
                pool.tensor_copy(ixs[:, c, :], src[:, bass.ds(STEP * j + RING * c, RING)]).then_inc(staged, 1)
                pool.wait_ge(staged, 2 * PH * t + 2 * j + c + 1)
                for r in range(RING):
                    pool.wait_ge(summed, base + RING * c + r + 1)
                    pool.sem_inc(passed, 1)
                    pool.indirect_dma_start(out=ring[:, r, :], out_offset=None, in_=dram["uv"],
                                            in_offset=bass.IndirectOffsetOnAxis(ap=ixs[:, c, r:r + 1], axis=0)).then_inc(slot[r], 16)
        pool.wait_ge(init, 2)
        pipeline(pool, nothing, step, nothing, nothing)

    @block.scalar
    def _(act):
        act.sem_inc(q_ev, CR)
        act.sem_inc(qt_ev, CR)
        act.sem_inc(s_ev, CR)
        act.sem_inc(p_ev, CR)
        act.sem_inc(geld, CR)
        act.wait_ge(cst, 80)
        act.wait_ge(init, 2)

        def pre(t, b, u):
            act.wait_ge(a_in, t - 1 + CR)
            act.dma_start(xm[b][:], dram["xm"][bass.ds(t, 1)].rearrange("o p n -> (o p) n")).then_inc(x_in[b], 16)
            act.wait_ge(dotted, SLOTS * (t - 1) + SLOTS + 1)
            act.wait_ge(x_in[b], 16 * u)
            act.activation(h2[b][:], xm[b][:], ACT.Square, accum_out=hss[:]).then_inc(p_sq, 1)
            act.wait_ge(p_sq, t + 1)
            act.activation(hstd[:], hss[:], ACT.Sqrt, bias=eps[:], scale=1.0 / D).then_inc(p_std, 1)
            act.wait_ge(q_mm, PH * t + CR)
            for n in range(2):
                act.wait_ge(p_t, 2 * t + n + 1)
                act.activation(h2T[:, 4 * n:4 * n + 4, :], TB[n][:], ACT.Copy).then_inc(p_ev, 1)

        def route(n, part):
            if part == 0:
                act.wait_ge(q_mm, n + 1 + CR)
                act.wait_ge(qt_t, n + CR)
                act.activation(qr[:], QR[:, 0:2 * DKEY], ACT.Copy).then_inc(q_ev, 1)
            if part == 1:
                act.wait_ge(qt_t, n + 1 + CR)
                act.wait_ge(s_mm, n + CR)
                act.activation(qT[:], TB[0][:, 0:2, :], ACT.Copy).then_inc(qt_ev, 1)
            if part == 2:
                act.wait_ge(s_mm, n + 1 + CR)
                act.wait_ge(routed, n + CR)
                act.activation(s1[:], SC[:, 0:2 * NKEY].rearrange("p (c k) -> p c k", c=2), ACT.Copy).then_inc(s_ev, 1)
            if part == 3:
                act.wait_ge(nmr, n + 1)
                act.activation(pe_[:], tv[:], ACT.Exp, bias=nmx[:], accum_out=psum_[:]).then_inc(ex, 1)

        def step(t, b, rt, rb, j):
            for q in range(STEP // GRP):
                if rt is not None:
                    if q < 3:
                        route(PH * rt + j, q)
                if t is not None:
                    slots(t, j, q, fold if rt is None else ident)
            if rt is not None:
                route(PH * rt + j, 3)

        def slots(t, j, q, matrix):
            base = SLOTS * t + STEP * j + GRP * q
            g = (SLOTS // GRP) * t + (STEP // GRP) * j + q
            act.wait_ge(dotted, base + GRP + 1 + SLOTS)
            act.wait_ge(cfd, g - 1 + CR)
            act.activation(gel[:, q % 2, :], dots[:, q % 2, :], ACT.Gelu).then_inc(geld, 1)
            act.wait_ge(cfd, g + 1 + CR)
            for n in range(GRP):
                r = (GRP * q + n) % RING
                act.wait_ge(summed, base + n + 1)
                act.activation(diag[:, r, :], matrix[:], ACT.Copy, scale=coef[:, q % 2, n:n + 1]).then_inc(dgd, 1)

        def finish(t, b):
            act.wait_ge(summed, SLOTS * t + (SLOTS if t is not TILES else SLOTS // COPIES) + RING)
            for n in range(2):
                act.activation(res[:, n * 512:(n + 1) * 512], acc[b][:, n, :], ACT.Copy).then_inc(a_ev, 1)
            act.wait_ge(a_ev, 2 * t + 2 + 2 * CR)
            if t is TILES:
                act.dma_start(io["y_s"], res[0:S_T, :]).then_inc(y_st, 16)
            else:
                act.dma_start(io["y_p"][bass.ts(t, P), :], res[:]).then_inc(y_st, 16)
            act.wait_ge(y_st, 16 * (t + 1))
        act.sem_inc(a_ev, 2 * CR)
        act.sem_inc(dgd, RING)
        pipeline(act, pre, step, nothing, finish)

    @block.tensor
    def _(pe):
        pe.sem_inc(summed, RING)
        pe.sem_inc(q_mm, CR)
        pe.sem_inc(qt_t, CR)
        pe.sem_inc(s_mm, CR)
        pe.sem_inc(a_in, CR)
        pe.wait_ge(cst, 80)
        pe.wait_ge(wld, 16)

        def pre(t, b, u):
            pe.wait_ge(p_h2, t + 1)
            pe.wait_ge(qt_ev, PH * t + CR)
            pe.wait_ge(p_ev, 2 * t + CR)
            pe.sem_inc(passed, 1)
            for n in range(2):
                for k in range(4):
                    tr = pe.transpose(TB[n][:, k, :], h2[b][:, (4 * n + k) * P:(4 * n + k + 1) * P], ident[:])
                tr.then_inc(p_t, 1)
            pe.wait_ge(p_ev, 2 * t + 2 + CR)

        def route(n, j, part):
            if part == 0:
                pe.wait_ge(q_ev, n + CR)
                pe.sem_inc(passed, 1)
                for k in range(KD):
                    mm = pe.matmul(QR[:, 0:2 * DKEY], h2T[:, k, :], w[:, k, bass.ts(j, 2 * DKEY)], start=(k == 0), stop=(k == KD - 1))
                mm.then_inc(q_mm, 1)
            if part == 1:
                pe.wait_ge(q_ev, n + 1 + CR)
                pe.wait_ge(qt_ev, n + CR)
                pe.sem_inc(passed, 1)
                for c in range(2):
                    tr = pe.transpose(TB[0][:, c, :], qr[:, c * DKEY:(c + 1) * DKEY], ident[:])
                tr.then_inc(qt_t, 1)
            if part == 2:
                pe.wait_ge(qt_ev, n + 1 + CR)
                pe.wait_ge(s_ev, n + CR)
                pe.sem_inc(passed, 1)
                for c in range(2):
                    mm = pe.matmul(SC[:, c * NKEY:(c + 1) * NKEY], qT[:, c, :], sub[:, bass.ds(2 * j + c, 1), :].rearrange("p o k -> p (o k)"),
                                   start=True, stop=True)
                mm.then_inc(s_mm, 1)

        def start(t, b):
            pe.wait_ge(a_ev, 2 * (t - 1) + 2 * CR)
            for n in range(2):
                mm = pe.matmul(acc[b][:, n, :], ident[:], xm[b][:, n * 512:(n + 1) * 512], start=True, stop=False, skip_group_check=True)
            mm.then_inc(a_in, 1)

        def step(t, b, rt, rb, j):
            for q in range(STEP // GRP):
                if rt is not None and q < 3:
                    route(PH * rt + j, j, q)
                if t is not None:
                    for n in range(GRP):
                        r = (GRP * q + n) % RING
                        pe.wait_ge(dgd, SLOTS * t + STEP * j + GRP * q + n + 1 + RING)
                        for c in range(2):
                            mm = pe.matmul(acc[b][:, c, :], diag[:, r, :], ring[:, r, D + c * 512:D + (c + 1) * 512], start=False, stop=False, skip_group_check=True)
                        mm.then_inc(summed, 1)

        def pre_and_start(t, b, u):
            pre(t, b, u)
            start(t, b)
        pipeline(pe, pre_and_start, step, nothing, nothing)

    @block.vector
    def _(dve):
        dve.memset(eps[:], EPS).then_inc(init, 1)
        dve.memset(cand2[:], 0.0).then_inc(init, 1)
        dve.sem_inc(dotted, SLOTS + 1)
        dve.sem_inc(cfd, CR)
        dve.sem_inc(routed, CR)
        dve.wait_ge(cst, 80)
        STEPS = 31

        def pre(t, b, u):
            dve.wait_ge(p_std, t + 1)
            dve.reciprocal(hrs[:], hstd[:]).then_inc(p_rs, 1)
            dve.wait_ge(p_rs, t + 1)
            dve.scalar_tensor_tensor(out=h2[b][:], in0=xm[b][:], scalar=hrs[:], in1=g2[:], op0=ALU.mult, op1=ALU.mult).then_inc(p_h2, 1)

        def route(n, rb, j):
            done = [0]

            def ready():
                dve.wait_ge(chain, STEPS * n + done[0])
                dve.sem_inc(passed, 1)

            def did(ins):
                done[0] += 1
                ins.then_inc(chain, 1)

            def top16(values, rest, v, i, count):
                for c in range(count):
                    did(dve.max(out=v(c)[:, 0:8], in_=values(c)))
                ready()
                for c in range(count):
                    did(dve.max_index(out=i(c)[:, 0:8], in_max=v(c)[:, 0:8], in_values=values(c)))
                    did(dve.match_replace(out=rest(c), in_to_replace=v(c)[:, 0:8], in_values=values(c), imm_value=NEG_FILL))
                ready()
                for c in range(count):
                    did(dve.max(out=v(c)[:, 8:16], in_=rest(c)))
                ready()
                for c in range(count):
                    did(dve.max_index(out=i(c)[:, 8:16], in_max=v(c)[:, 8:16], in_values=rest(c)))
                ready()
            dve.wait_ge(s_ev, n + 1 + CR)
            dve.sem_inc(passed, 1)
            top16(lambda c: s1[:, c, :], lambda c: s2[:, c, :], lambda c: kv[:, c, :], lambda c: ki[:, c, :], 2)
            did(dve.tensor_tensor(cand[:], kv[:, 0, :].unsqueeze(2).to_broadcast([P, TOPK, TOPK]),
                                  kv[:, 1, :].unsqueeze(1).to_broadcast([P, TOPK, TOPK]), ALU.add))
            did(dve.tensor_copy(kf[:], ki[:]))
            ready()
            flat = cand[:].rearrange("p a b -> p (a b)")
            flat2 = cand2[:].rearrange("p a b -> p (a b)")
            top16(lambda c: flat, lambda c: flat2, lambda c: tv[:], lambda c: ti[:], 1)
            did(dve.tensor_scalar(nmx[:], tv[:, 0:1], -1.0, None, ALU.mult))
            did(dve.tensor_scalar(ab[:, 0, :], ti[:], 4, None, ALU.logical_shift_right))
            did(dve.tensor_scalar(ab[:, 1, :], ti[:], TOPK - 1, None, ALU.bitwise_and))
            ready()
            dve.sem_inc(nmr, 1)
            did(dve.tensor_copy(abf[:], ab[:]))
            ready()
            did(dve.tensor_tensor(hot[:], abf[:].unsqueeze(3).to_broadcast([P, 2, TOPK, TOPK]),
                                  iota[:].unsqueeze(1).unsqueeze(1).to_broadcast([P, 2, TOPK, TOPK]), ALU.is_equal))
            ready()
            did(dve.tensor_tensor(hot[:], hot[:], kf[:].unsqueeze(2).to_broadcast([P, 2, TOPK, TOPK]), ALU.mult))
            ready()
            did(dve.tensor_reduce(pick[:], hot[:], AX.X, ALU.add))
            ready()
            did(dve.scalar_tensor_tensor(out=idx[rb][:, bass.ts(j, TOPK)], in0=pick[:, 0, :], scalar=float(NKEY), in1=pick[:, 1, :],
                                         op0=ALU.mult, op1=ALU.add))
            dve.wait_ge(ex, n + 1)
            did(dve.reciprocal(pinv[:], psum_[:]))
            ready()
            did(dve.tensor_scalar(gw[rb][:, bass.ts(j, TOPK)], pe_[:], pinv[:], None, ALU.mult))
            ready()
            dve.sem_inc(routed, 1)
            while done[0] < STEPS:
                dve.sem_inc(chain, 1)
                done[0] += 1
            assert done[0] == STEPS

        def dot(t, b, j, q):
            base = SLOTS * t + STEP * j + GRP * q
            g = (SLOTS // GRP) * t + (STEP // GRP) * j + q
            dve.wait_ge(geld, g - 1 + CR)
            for n in range(GRP):
                r = (GRP * q + n) % RING
                dve.wait_ge(slot[r], 16 * ((SLOTS // RING) * t + 2 * j + (GRP * q) // RING + 1))
                dve.tensor_tensor_reduce(out=ring[:, r, 0:D], in0=ring[:, r, 0:D], in1=h2[b][:], scale=1.0, scalar=0.0,
                                         op0=ALU.mult, op1=ALU.add, accum_out=dots[:, q % 2, n:n + 1]).then_inc(dotted, 1)

        def weigh(t, b, j, q, weights):
            base = SLOTS * t + STEP * j + GRP * q
            g = (SLOTS // GRP) * t + (STEP // GRP) * j + q
            dve.wait_ge(geld, g + 1 + CR)
            dve.wait_ge(dgd, base - GRP + RING)
            dve.tensor_tensor(coef[:, q % 2, :], gel[:, q % 2, :], weights[:, bass.ds(STEP * j + GRP * q, GRP)], ALU.mult).then_inc(cfd, 1)

        def step(t, b, rt, rb, j):
            if t is not None:
                weights = gw_s if rt is None else gw[b]
                for q in range(STEP // GRP):
                    dot(t, b, j, q)
                    weigh(t, b, j, q, weights)
            if rt is not None:
                route(PH * rt + j, rb, j)

        def last():
            dve.wait_ge(routed, PH * ALL + CR)
            n = SLOTS // COPIES
            for c in range(COPIES):
                p = slice(c * S_T, (c + 1) * S_T)
                dve.tensor_copy(idx_s[p, :], idx[0][p, c * n:(c + 1) * n]).then_inc(spread, 1)
                dve.tensor_copy(gw_s[p, :], gw[0][p, c * n:(c + 1) * n]).then_inc(spread, 1)
            dve.wait_ge(spread, 2 * COPIES)
        pipeline(dve, pre, step, last, nothing)


def program(nc, io, dram):
    with ExitStack() as ctx:
        mix_phase(nc, ctx, io, dram, None)
    with ExitStack() as ctx:
        attend_phase(nc, ctx, io, dram)
    with ExitStack() as ctx:
        peer_phase(nc, ctx, io, dram)


_WEIGHTS = ["g_norm1", "w_in", "w_gla_a2", "b_gla_a", "g_gla_onorm", "g_fox_qnorm", "g_fox_knorm", "b_fox_f",
            "w_out", "g_norm2", "w_peer_q"]


def kernel(**inputs):
    import numpy as np
    import concourse.bacc as bacc
    from concourse.bass_utils import run_bass_kernel_spmd

    nc = bacc.Bacc("TRN2", target_bir_lowering=False, num_devices=1)
    arrays = {}

    def inp(name, a):
        a = np.ascontiguousarray(a)
        arrays["in_" + name] = a
        return nc.dram_tensor("in_" + name, a.shape, mybir.dt.from_np(a.dtype), kind="ExternalInput").ap()

    def out(name, shape):
        return nc.dram_tensor("out_" + name, shape, F32, kind="ExternalOutput").ap()

    x = {k: np.asarray(v) for k, v in inputs.items()}
    io = {name: inp(name, x[name]) for name in _WEIGHTS}
    io["cache_fox_logf"] = inp("cache_fox_logf", x["cache_fox_logf"])
    io["state_gla"] = inp("state_gla", x["state_gla"][0, 0])
    for s, n in (("p", T), ("s", S_T)):
        io[s + "_fox_k"] = out(s + "_fox_k", (n, FH * FD))
        io[s + "_fox_v"] = out(s + "_fox_v", (n, FH * FD))
        io[s + "_fox_logf"] = out(s + "_fox_logf", (n, FH))
        io[s + "_state"] = out(s + "_state", (GH, GK, GV))
        io["y_" + s] = out("y_" + s, (n, D))

    rows = np.concatenate([x["x_prompt"][0]] + [x["x_sample"][0]] * COPIES).reshape(ALL, P, D)
    dram = {
        "xr": inp("x_rows", rows),
        "xT": inp("x_T", rows.reshape(ALL, P, KD, P).transpose(0, 3, 2, 1).reshape(ALL, P, D)),
    }
    dram["uv"] = inp("peer_uv", np.concatenate([x["peer_u"][0], x["peer_v"][0]], axis=1))
    dram["subkeys_T"] = inp("subkeys_T", x["peer_subkeys"][0].transpose(3, 0, 1, 2).reshape(P, PH * 2, NKEY))
    dram["iota"] = inp("iota16", np.tile(np.arange(TOPK, dtype=np.float32), (P, 1)))
    dram["fold"] = inp("fold_copies", (np.arange(P)[:, None] % S_T == np.arange(P)[None, :] % S_T).astype(np.float32))
    dram["g1"] = inp("g_norm1_T", x["g_norm1"].reshape(KD, P).T)
    s, t = np.arange(P)[:, None], np.arange(P)[None, :]
    tri = np.stack([s <= t, (s <= t) & (s // S_T == t // S_T)], axis=1)
    level = [(s // (2 * h) == t // (2 * h)) & (s % (2 * h) < h) & (t % (2 * h) >= h) for h in LEVELS] + [s == t]
    n, m = np.arange(PB * FH)[:, None], np.arange(PB * FH)[None, :]
    before = (n % FH == m % FH) & (n // FH < m // FH)
    dram["ident"] = inp("ident", np.eye(P, dtype=np.float32))
    dram["tri"] = inp("tri", tri.astype(np.float32))
    dram["masks"] = inp("level_masks", np.stack(level, axis=1).astype(np.uint32))
    dram["earlier"] = inp("earlier_blocks", np.concatenate([before, n % FH == np.arange(FH)[None, :]], axis=1).astype(np.float32))
    import ml_dtypes
    dram["ident_b"] = inp("ident_bf16", np.eye(P, dtype=ml_dtypes.bfloat16))
    dram["causal"] = inp("causal_neg", (np.stack([t > s, t > s % S_T], axis=1) * NEG).astype(ml_dtypes.bfloat16))
    dram["kT_past"] = inp("past_k_T", x["cache_fox_k"][0, 0].transpose(2, 1, 0))
    io["cache_fox_v"] = inp("cache_fox_v", x["cache_fox_v"].reshape(PAST, FH * FD))
    for name, shape in (("xm", (ALL, P, D)), ("q", (ALL, P, FH * FD)), ("mixg", (ALL, P, GH * GV)), ("negc", (FH, ALL * P)), ("negc_past", (PB * FH, P))):
        dram[name] = nc.dram_tensor("scratch_" + name, shape, F32).ap()
    program(nc, io, dram)
    r = run_bass_kernel_spmd(nc, [arrays], core_ids=[0]).results[0]

    def got(name, *shape):
        return r["out_" + name].reshape(shape)

    return (got("y_p", 1, T, D), got("y_s", 1, S_T, D),
            got("p_fox_k", 1, 1, T, FH, FD), got("p_fox_v", 1, 1, T, FH, FD), got("p_fox_logf", 1, 1, T, FH),
            got("p_state", 1, 1, GH, GK, GV),
            got("s_fox_k", 1, 1, S_T, FH, FD), got("s_fox_v", 1, 1, S_T, FH, FD), got("s_fox_logf", 1, 1, S_T, FH),
            got("s_state", 1, 1, GH, GK, GV))
```

```python
from contextlib import ExitStack

import concourse.bass as bass
from concourse import mybir

F32 = mybir.dt.float32
BF16 = mybir.dt.bfloat16
U32 = mybir.dt.uint32
ALU = mybir.AluOpType
ACT = mybir.ActivationFunctionType
AX = mybir.AxisListType

P = 128
D = 1024
KD = D // P
T = 1024
TILES = T // P
ALL = TILES + 1
S_T = 32
COPIES = P // S_T
PAST = 1024
PB = PAST // P
EPS = 1e-6

GH, GK, GV, LR = 4, 64, 128, 16
FH, FD = 8, 64
GATE_NORM = 16.0
FOX_SCALE = FD ** -0.5
GLA_SCALE = GK ** -0.5

C_QK, C_GV, C_GG = 0, 2 * GH * GK, 2 * GH * GK + GH * GV
C_LR = C_GG + GH * GV
C_FQ = C_LR + LR
C_FK, C_FV = C_FQ + FH * FD, C_FQ + 2 * FH * FD
C_FF = C_FQ + 3 * FH * FD
WIN = C_FF + FH
GATES = GH * GK

PH, NKEY, DKEY, TOPK = 8, 128, 128, 16
SLOTS = PH * TOPK
LEVELS = [64, 32, 16, 8, 4, 2, 1]
NEG = -1.0e30
NEG_FILL = -3.0e38


def wait(eng, sem, count):
    if not isinstance(count, int) or count > 0:
        eng.wait_ge(sem, count)


def mix_phase(nc, ctx, io, dram):
    def sb(n, s, d=F32):
        return ctx.enter_context(nc.sbuf_tensor(n, s, d))

    def ps(n, s, d=F32):
        return ctx.enter_context(nc.psum_tensor(n, s, d))

    w = sb("w_in", [P, KD, WIN])
    g1 = sb("g_norm1", [P, KD])
    ident = sb("ident", [P, P])
    tri = sb("tri", [P, 2, P])
    masks = sb("level_masks", [P, len(LEVELS) + 1, P], U32)
    wa = sb("w_gate", [LR, GATES])
    ba = sb("b_gate", [1, GATES])
    ones = sb("ones_row", [1, P])
    bf = sb("b_forget", [P, FH])
    gon = sb("g_out_norm", [P, GV])
    gqk = sb("g_qk_norm", [P, 2, FD])
    eps = sb("eps_mix", [P, 1])

    xT = [sb(f"x_T{b}", [P, KD, P]) for b in range(2)]
    xr = [sb(f"x_rows{b}", [P, D]) for b in range(2)]
    ss = sb("x_sumsq", [P, 1])
    std = sb("x_std", [P, 1])
    rstd = [sb(f"x_rstd{b}", [P, 1]) for b in range(2)]
    zqk = [sb(f"z_gla_qk{b}", [P, 512]) for b in range(2)]
    zv = [sb(f"z_gla_v{b}", [P, 512]) for b in range(2)]
    zg = [sb(f"z_gla_g{b}", [P, 512]) for b in range(2)]
    zs = [sb(f"z_small{b}", [P, LR + FH]) for b in range(2)]
    fqk = [sb(f"fox_qk{b}", [P, 2, 512]) for b in range(2)]
    fv = [sb(f"fox_v{b}", [P, 512]) for b in range(2)]
    lrT = sb("lowrank_T", [LR, P])
    gx = sb("gate_logits", [P, GATES + FH])
    ga = sb("gate_abs", [P, GATES + FH])
    ge = sb("gate_exp", [P, GATES + FH])
    gl = sb("gate_ln", [P, GATES + FH])
    ls = [sb(f"log_gates{b}", [P, GATES + FH]) for b in range(2)]
    nc_T = [sb(f"neg_c_T{b}", [FH, P]) for b in range(2)]
    carry = sb("neg_c_carry", [FH, 1])
    pastf = sb("past_logf", [P, PB * FH])
    past_sum = sb("past_block_sums", [PB * FH, 1])
    past_carry = sb("past_block_carry", [PB * FH, 1])
    past_nc = sb("past_neg_c", [PB * FH, P])
    earlier = sb("earlier_blocks", [PB * FH, PB * FH + FH])
    qT = sb("gla_q_T", [GK, GH, P])
    kT = sb("gla_k_T", [GK, GH, P])
    bT = sb("b_T", [GK, GH, P])
    eb = sb("exp_b", [GK, GH, P])
    ekd = sb("exp_last_minus_b", [GK, GH, P])
    qe = sb("q_exp_b", [GK, GH, P])
    kd = sb("k_decayed_T", [GK, GH, P])
    kdr = sb("k_decayed", [P, 2 * P])
    lev = sb("level_exp", [GK, len(LEVELS), GH, P])
    lq = [sb(f"level_q{b}", [GK, GH, P]) for b in range(2)]
    lk = [sb(f"level_k{b}", [GK, GH, P]) for b in range(2)]
    AT = sb("A_T", [P, GH, P])
    S = sb("gla_state", [GK, GH, GV])
    osq = sb("o_squared", [P, GH, GV])
    oss = sb("o_sumsq", [P, GH])
    ostd = sb("o_std", [P, GH])
    ors = sb("o_rstd", [P, GH])
    mixg = [sb(f"mix_gla{b}", [P, GH * GV]) for b in range(2)]
    fsq = sb("fox_squared", [P, 2, 512])
    fss = sb("fox_sumsq", [P, 2 * FH])
    fstd = sb("fox_std", [P, 2 * FH])
    frs = sb("fox_rstd", [P, 2 * FH])

    Z = [ps(f"ps_z{b}", [P, 512]) for b in range(2)]
    G = ps("ps_gate_ds", [P, 512])
    C = ps("ps_cumsum", [P, 512])
    TQ = ps("ps_q_T_level", [P, GH, P])
    TK = ps("ps_k_T", [P, GH, P])
    LP = [ps("ps_level", [P, GH, P]), TQ]
    O = ps("ps_o", [P, GH, GV])
    la_ps, cT_ps, lrT_ps = G[:, 0:GATES], G[0:FH, 256:384], G[0:LR, 384:512]
    bT_ps = ds_ps = C[0:GK, :].rearrange("p (h v) -> p h v", h=GH)
    kdr_ps = TK[:, 0:2, :].rearrange("p a t -> p (a t)")

    CH = [(C_LR, LR), (C_QK, 512), (C_GV, 512), (C_GG, 512), (C_FQ, 512), (C_FK, 512), (C_FV, 512)]
    NCH = len(CH)
    SMALL, QK, VV, GG, FQ, FK, FV = range(NCH)

    def sem(n):
        return ctx.enter_context(nc.semaphore(n))

    cst = sem("mix_consts_loaded")
    past_in = sem("past_logf_loaded")
    w_ld = [sem(f"w_in_loaded{k}") for k in range(KD)]
    w_sc = sem("w_in_scaled")
    inited = sem("mix_inited")
    x_in = [sem(f"x_loaded{b}") for b in range(2)]
    x_sq = sem("x_squared")
    x_std = sem("x_std_ready")
    x_rs = sem("x_rstd_ready")
    z_mm = sem("z_projected")
    z_ev = sem("z_in_sbuf")
    lr_t = sem("lowrank_transposed")
    lr_ev = sem("lowrank_T_ready")
    la_mm = sem("gate_projected")
    gx_r = sem("gate_logits_ready")
    g_abs = sem("gate_abs_ready")
    g_exp = sem("gate_exp_ready")
    g_ln = sem("gate_ln_ready")
    ls_r = sem("log_gates_ready")
    cum = sem("cumsums_done")
    b_r = sem("b_T_ready")
    c_r = sem("neg_c_ready")
    c_c = sem("neg_c_carried")
    past_mm = sem("past_cumsum_done")
    past_s = sem("past_sums_ready")
    past_c = sem("past_carry_done")
    past_r = sem("past_neg_c_ready")
    past_st = sem("past_neg_c_stored")
    qk_t = sem("gla_qk_transposed")
    qk_ev = sem("gla_qk_T_ready")
    eb_r = sem("exp_b_ready")
    qekd = sem("q_exp_b_k_decayed_ready")
    arg = sem("level_args_ready")
    lexp = sem("level_exps_ready")
    lqk = sem("level_qk_ready")
    lmm = sem("level_products_done")
    lsel = sem("level_selected")
    at0 = sem("A_T_cleared")
    kd_t = sem("k_decayed_transposed")
    kd_ev = sem("k_decayed_rows_ready")
    o_mm = sem("o_done")
    ds_mm = sem("state_step_done")
    s_up = sem("state_updated")
    s_ld = sem("sample_state_loaded")
    o_sq = sem("o_squares_done")
    o_std = sem("o_std_ready")
    o_rs = sem("o_rstd_ready")
    silu = sem("silu_ready")
    sg = sem("silu_g_ready")
    mixd = sem("mix_gla_ready")
    f_sq = sem("fox_squares_done")
    f_ss = sem("fox_sumsq_done")
    f_std = sem("fox_std_ready")
    f_rs = sem("fox_rstd_ready")
    f_n = sem("fox_scaled")
    f_g = sem("fox_normed")
    stored = sem("mix_stores_landed")
    flushed = sem("mix_tiles_flushed")
    s_st = sem("gla_states_landed")
    passed = sem("mix_waits_passed")

    LV = len(LEVELS)
    NL = LV + 1
    s_levels = [l for l, half in enumerate(LEVELS) if half < S_T]

    def levels(sample):
        return s_levels if sample else list(range(LV))

    def last(sample):
        return S_T if sample else P

    def over_tiles(eng, tile, prompt_done=None):
        for b in range(2):
            tile(b, b, 1, False)
        with eng.Fori(1, TILES // 2) as i:
            for b in range(2):
                tile(2 * i + b, b, i + 1, False)
        if prompt_done:
            prompt_done()
        tile(TILES, 0, TILES // 2 + 1, True)

    block = ctx.enter_context(nc.Block())

    @block.sync
    def _(sp):
        for dst, src in ((g1[:], dram["g1"]), (ident[:], dram["ident"]),
                         (tri[:], dram["tri"]), (masks[:], dram["masks"]), (wa[:], io["w_gla_a2"][0]),
                         (ba[:], io["b_gla_a"]), (bf[:], io["b_fox_f"].to_broadcast([P, FH])),
                         (gon[:], io["g_gla_onorm"].to_broadcast([P, GV])),
                         (gqk[:, 0, :], io["g_fox_qnorm"].to_broadcast([P, FD])),
                         (gqk[:, 1, :], io["g_fox_knorm"].to_broadcast([P, FD])),
                         (earlier[:], dram["earlier"])):
            sp.dma_start(dst, src).then_inc(cst, 16)
        for k in range(KD):
            sp.dma_start(w[:, k, :], io["w_in"][0, k * P:(k + 1) * P, :]).then_inc(w_ld[k], 16)
        sp.dma_start(pastf[:].rearrange("p (n h) -> p n h", h=FH),
                     io["cache_fox_logf"][0, 0].rearrange("(n p) h -> p n h", p=P)).then_inc(past_in, 16)

    @block.gpsimd
    def _(pool):
        def load(t, b):
            pool.dma_start(xT[b][:].rearrange("p k t -> p (k t)"), dram["xT"][bass.ds(t, 1)].rearrange("o p n -> (o p) n")).then_inc(x_in[b], 16)
            pool.dma_start(xr[b][:], dram["xr"][bass.ds(t, 1)].rearrange("o p n -> (o p) n")).then_inc(x_in[b], 16)

        def stores(t, b, u, sample):
            out = "s" if sample else "p"
            rows = last(sample)

            def at(name):
                return io[out + name] if sample else io[out + name][bass.ts(t, P), :]

            def scratch(name):
                return dram[name][bass.ds(t, 1)].rearrange("o p n -> (o p) n")
            if not sample:
                wait(pool, z_mm, t * NCH)
                wait(pool, x_sq, t)
                pool.sem_inc(passed, 1)
                load(t + 1, 1 - b)
            wait(pool, ls_r, t + 1)
            pool.sem_inc(passed, 1)
            pool.dma_start(at("_fox_logf"), ls[b][0:rows, GATES:GATES + FH]).then_inc(stored, 16)
            wait(pool, c_r, t + 1)
            pool.sem_inc(passed, 1)
            pool.dma_start(dram["negc"][:, bass.ts(t, P)], nc_T[b][:]).then_inc(stored, 16)
            wait(pool, z_ev, NCH * (t + 1))
            pool.sem_inc(passed, 1)
            pool.dma_start(at("_fox_v"), fv[b][0:rows, :]).then_inc(stored, 16)
            wait(pool, f_g, 2 * (t + 1))
            pool.sem_inc(passed, 1)
            pool.dma_start(at("_fox_k"), fqk[b][0:rows, 1, :]).then_inc(stored, 16)
            pool.dma_start(scratch("q"), fqk[b][:, 0, :]).then_inc(stored, 16)
            wait(pool, mixd, GH * (t + 1))
            pool.sem_inc(passed, 1)
            pool.dma_start(scratch("mixg"), mixg[b][:]).then_inc(stored, 16)
            wait(pool, stored, 96 * (t + 1))
            pool.sem_inc(flushed, 1)

        def swap_state():
            pool.wait_ge(s_up, GH * TILES)
            pool.dma_start(io["p_state"].rearrange("h k v -> k h v"), S[:]).then_inc(s_st, 16)
            pool.wait_ge(s_st, 16)
            pool.dma_start(S[:], io["state_gla"].rearrange("h k v -> k h v")).then_inc(s_ld, 16)
            pool.wait_ge(past_r, 1)
            pool.dma_start(dram["negc_past"], past_nc[:]).then_inc(past_st, 16)
        load(0, 0)
        over_tiles(pool, stores, swap_state)
        pool.wait_ge(s_up, GH * ALL)
        pool.dma_start(io["s_state"].rearrange("h k v -> k h v"), S[:]).then_inc(s_st, 16)
        pool.wait_ge(s_st, 32)
        pool.wait_ge(past_st, 16)

    @block.scalar
    def _(act):
        def tile(t, b, u, sample):
            n_last = last(sample)
            lv = levels(sample)
            wait(act, x_in[b], 32 * u)
            act.activation(xr[b][:], xr[b][:], ACT.Square, accum_out=ss[:]).then_inc(x_sq, 1)
            wait(act, x_sq, t + 1)
            act.activation(std[:], ss[:], ACT.Sqrt, bias=eps[:], scale=1.0 / D).then_inc(x_std, 1)
            wait(act, x_rs, t + 1)
            wait(act, flushed, t - 1)

            def evac(c, dst):
                wait(act, z_mm, t * NCH + c + 1)
                act.activation(dst, Z[c % 2][:, 0:dst.shape[-1]], ACT.Copy, scale=rstd[b][:]).then_inc(z_ev, 1)
            evac(SMALL, zs[b][:])
            evac(QK, zqk[b][:])
            wait(act, lr_t, t + 1)
            act.activation(lrT[:], lrT_ps, ACT.Copy).then_inc(lr_ev, 1)
            evac(VV, zv[b][:])
            wait(act, qk_t, t + 1)
            act.activation(qT[:], TQ[0:GK], ACT.Copy, scale=GLA_SCALE).then_inc(qk_ev, 1)
            act.activation(kT[:], TK[0:GK], ACT.Copy).then_inc(qk_ev, 1)
            wait(act, gx_r, 2 * (t + 1))
            act.activation(ga[:], gx[:], ACT.Abs).then_inc(g_abs, 1)
            wait(act, g_abs, t + 1)
            act.activation(ge[:], ga[:], ACT.Exp, scale=-1.0).then_inc(g_exp, 1)
            wait(act, g_exp, t + 1)
            act.activation(gl[:], ge[:], ACT.Ln, bias=1.0).then_inc(g_ln, 1)
            evac(GG, zg[b][:])
            evac(FQ, fqk[b][:, 0, :])
            wait(act, b_r, t + 1)
            wait(act, s_up, GH * t)
            act.activation(eb[:], bT[:], ACT.Exp).then_inc(eb_r, 1)
            for h in range(GH):
                act.activation(ekd[:, h, :], bT[:, h, :], ACT.Exp, bias=bT[:, h, n_last - 1:n_last], scale=-1.0).then_inc(eb_r, 1)
            evac(FK, fqk[b][:, 1, :])
            evac(FV, fv[b][:])
            wait(act, arg, 2 * LV * t + 2 * len(lv))
            act.activation(lev[:, lv[0]:, :, :], lev[:, lv[0]:, :, :], ACT.Exp).then_inc(lexp, 1)
            wait(act, z_ev, t * NCH + GG + 1)
            act.activation(zg[b][:], zg[b][:], ACT.Silu).then_inc(silu, 1)
            wait(act, f_ss, t + 1)
            act.activation(fstd[:], fss[:], ACT.Sqrt, bias=eps[:], scale=1.0 / FD).then_inc(f_std, 1)
            wait(act, kd_t, t + 1)
            act.activation(kdr[:], kdr_ps, ACT.Copy).then_inc(kd_ev, 1)
            wait(act, o_mm, t + 1)
            for h in range(GH):
                act.activation(osq[:, h, :], O[:, h, :], ACT.Square, accum_out=oss[:, h:h + 1]).then_inc(o_sq, 1)
            wait(act, o_sq, GH * (t + 1))
            act.activation(ostd[:], oss[:], ACT.Sqrt, bias=eps[:], scale=1.0 / GV).then_inc(o_std, 1)

        act.wait_ge(inited, 1)
        over_tiles(act, tile)

    @block.tensor
    def _(pe):
        def tile(t, b, u, sample):
            kind = 1 if sample else 0
            lv = levels(sample)

            def project(c):
                wait(pe, z_ev, t * NCH + c - (1 if c else 0))
                off, n = CH[c]
                for k in range(KD):
                    if isinstance(t, int) and t == 0:
                        pe.wait_ge(w_sc, k + 1)
                    if c == SMALL:
                        pe.matmul(Z[0][:, 0:LR], xT[b][:, k, :], w[:, k, C_LR:C_LR + LR], start=(k == 0), stop=False, skip_group_check=True)
                        m = pe.matmul(Z[0][:, LR:LR + FH], xT[b][:, k, :], w[:, k, C_FF:C_FF + FH], start=False, stop=(k == KD - 1), skip_group_check=True)
                    else:
                        m = pe.matmul(Z[c % 2][:, 0:n], xT[b][:, k, :], w[:, k, off:off + n], start=(k == 0), stop=(k == KD - 1))
                m.then_inc(z_mm, 1)
            wait(pe, x_in[b], 32 * u)
            project(SMALL)
            project(QK)
            wait(pe, z_ev, t * NCH + SMALL + 1)
            wait(pe, c_r, t)
            pe.transpose(lrT_ps, zs[b][:, 0:LR], ident[:]).then_inc(lr_t, 1)
            project(VV)
            wait(pe, lr_ev, t + 1)
            pe.matmul(la_ps, lrT[:], wa[:], start=True, stop=False)
            pe.matmul(la_ps, ones[:], ba[:], start=False, stop=True).then_inc(la_mm, 1)
            wait(pe, z_ev, t * NCH + QK + 1)
            wait(pe, kd_ev, t)
            wait(pe, lsel, NL * t)
            pe.sem_inc(passed, 1)
            for h in range(2 * GH):
                m = pe.transpose((TQ if h < GH else TK)[0:GK, h % GH, :], zqk[b][:, h * GK:(h + 1) * GK], ident[:])
            m.then_inc(qk_t, 1)
            project(GG)
            project(FQ)
            wait(pe, ls_r, t + 1)
            wait(pe, s_up, GH * t)
            for h in range(GH):
                pe.matmul(bT_ps[:, h, :], ls[b][:, h * GK:(h + 1) * GK], tri[:, kind, :], start=True, stop=True)
            pe.matmul(cT_ps, ls[b][:, GATES:GATES + FH], tri[:, kind, :], start=True, stop=True).then_inc(cum, 1)
            project(FK)
            project(FV)
            for n, l in enumerate([None] + lv):
                wait(pe, lsel, NL * t + n - 1)
                if n == 0:
                    wait(pe, qk_ev, 2 * (t + 1))
                    kk, qq = kT, qT
                else:
                    wait(pe, lqk, 2 * LV * t + 2 * n)
                    kk, qq = lk[n % 2], lq[n % 2]
                for h in range(GH):
                    m = pe.matmul(LP[n % 2][:, h, :], kk[:, h, :], qq[:, h, :], start=True, stop=True)
                m.then_inc(lmm, 1)
            wait(pe, qekd, 2 * (t + 1))
            wait(pe, qk_ev, 2 * (t + 1))
            pe.sem_inc(passed, 1)
            for h in range(GH):
                m = pe.transpose(kdr_ps[:, h * GK:(h + 1) * GK], kd[:, h, :], ident[0:GK, 0:GK])
            m.then_inc(kd_t, 1)
            wait(pe, lsel, NL * t + 1 + len(lv))
            wait(pe, mixd, GH * t)
            wait(pe, s_up, GH * t)
            wait(pe, z_ev, t * NCH + VV + 1)
            if sample:
                pe.wait_ge(s_ld, 16)
            for h in range(GH):
                pe.matmul(O[:, h, :], AT[:, h, :], zv[b][:, h * GV:(h + 1) * GV], start=True, stop=False)
                m = pe.matmul(O[:, h, :], qe[:, h, :], S[:, h, :], start=False, stop=True)
            m.then_inc(o_mm, 1)
            wait(pe, kd_ev, t + 1)
            n = last(sample)
            for h in range(GH):
                m = pe.matmul(ds_ps[:, h, :], kdr[0:n, h * GK:(h + 1) * GK], zv[b][0:n, h * GV:(h + 1) * GV], start=True, stop=True)
            m.then_inc(ds_mm, 1)

        def past():
            pe.wait_ge(past_in, 16)
            pe.wait_ge(s_up, GH * TILES)
            pe.matmul(C[0:PB * FH, 0:P], pastf[:], tri[:, 0, :], start=True, stop=True).then_inc(past_mm, 1)
            pe.wait_ge(past_s, 1)
            pe.matmul(C[0:PB * FH, 128:129], earlier[:, 0:PB * FH], past_sum[:], start=True, stop=True, skip_group_check=True)
            pe.matmul(C[0:FH, 256:257], earlier[:, PB * FH:], past_sum[:], start=True, stop=True, skip_group_check=True).then_inc(past_c, 1)
            pe.wait_ge(past_r, 2)
        pe.wait_ge(cst, 16 * 11)
        over_tiles(pe, tile, past)

    @block.vector
    def _(dve):
        def tile(t, b, u, sample):
            n_last = last(sample)
            lv = levels(sample)
            wait(dve, x_std, t + 1)
            dve.reciprocal(rstd[b][:], std[:]).then_inc(x_rs, 1)
            wait(dve, flushed, t - 1)
            wait(dve, z_ev, t * NCH + SMALL + 1)
            wait(dve, ls_r, t)
            dve.tensor_tensor(gx[:, GATES:], zs[b][:, LR:], bf[:], ALU.add).then_inc(gx_r, 1)
            wait(dve, la_mm, t + 1)
            dve.tensor_copy(gx[:, 0:GATES], la_ps).then_inc(gx_r, 1)
            wait(dve, o_mm, t)
            dve.memset(AT[:], 0.0).then_inc(at0, 1)
            wait(dve, g_ln, t + 1)
            dve.scalar_tensor_tensor(out=ls[b][:], in0=gx[:], scalar=0.0, in1=gl[:], op0=ALU.min, op1=ALU.subtract).then_inc(ls_r, 1)
            wait(dve, cum, t + 1)
            wait(dve, c_c, t + 1)
            dve.tensor_scalar(nc_T[b][:], cT_ps, -1.0, carry[:], ALU.mult, ALU.add).then_inc(c_r, 1)
            wait(dve, c_r, t + 1)
            dve.tensor_copy(carry[:], nc_T[b][:, n_last - 1:n_last]).then_inc(c_c, 1)
            wait(dve, eb_r, 5 * t)
            dve.tensor_scalar(bT[:], bT_ps, 1.0 / GATE_NORM, None, ALU.mult).then_inc(b_r, 1)
            wait(dve, b_r, t + 1)
            for l in lv:
                half = LEVELS[l]
                bb = bT[:].rearrange("p i (n a x) -> p (i n) a x", a=2, x=half)
                mid = bb[:, :, 0, half - 1:half].to_broadcast([GK, bb.shape[1], half])
                ll = lev[:, l, :, :].rearrange("p i (n a x) -> p (i n) a x", a=2, x=half)
                wait(dve, lqk, 2 * LV * t)
                dve.tensor_tensor(ll[:, :, 1, :], bb[:, :, 1, :], mid, ALU.subtract).then_inc(arg, 1)
                dve.tensor_tensor(ll[:, :, 0, :], mid, bb[:, :, 0, :], ALU.subtract).then_inc(arg, 1)
            wait(dve, eb_r, 5 * (t + 1))
            wait(dve, qk_ev, 2 * (t + 1))
            wait(dve, kd_t, t)
            dve.tensor_tensor(qe[:], qT[:], eb[:], ALU.mult).then_inc(qekd, 1)
            dve.tensor_tensor(kd[:], kT[:], ekd[:], ALU.mult).then_inc(qekd, 1)
            wait(dve, lexp, t + 1)
            wait(dve, at0, t + 1)

            def select(n, l):
                wait(dve, lmm, NL * t + n + 1)
                wait(dve, lsel, NL * t + n)
                dve.sem_inc(passed, 1)
                dve.copy_predicated(AT[:], masks[:, l, :].unsqueeze(1).to_broadcast([P, GH, P]), LP[n % 2][:]).then_inc(lsel, 1)
            for n, l in enumerate(lv):
                half = LEVELS[l]

                def view(x, a):
                    return x.rearrange("p i (n a x) -> p (i n) a x", a=2, x=half)[:, :, a, :]
                wait(dve, lmm, NL * t + n)
                o = (n + 1) % 2
                wait(dve, lqk, 2 * LV * t + 2 * n)
                dve.tensor_tensor(view(lq[o][:], 1), view(qT[:], 1), view(lev[:, l, :, :], 1), ALU.mult).then_inc(lqk, 1)
                dve.tensor_tensor(view(lk[o][:], 0), view(kT[:], 0), view(lev[:, l, :, :], 0), ALU.mult).then_inc(lqk, 1)
                select(n, lv[n - 1] if n else LV)
            select(len(lv), lv[-1])
            wait(dve, silu, t + 1)
            dve.tensor_tensor(zg[b][:].rearrange("p (h v) -> p h v", h=GH), zg[b][:].rearrange("p (h v) -> p h v", h=GH),
                              gon[:].unsqueeze(1).to_broadcast([P, GH, GV]), ALU.mult).then_inc(sg, 1)
            wait(dve, z_ev, t * NCH + FK + 1)
            wait(dve, f_ss, t)
            dve.tensor_tensor(fsq[:], fqk[b][:], fqk[b][:], ALU.mult).then_inc(f_sq, 1)
            wait(dve, f_sq, t + 1)
            dve.tensor_reduce(fss[:], fsq[:].rearrange("p c (h d) -> p (c h) d", d=FD), AX.X, ALU.add).then_inc(f_ss, 1)
            wait(dve, f_std, t + 1)
            dve.reciprocal(frs[:], fstd[:]).then_inc(f_rs, 1)
            wait(dve, f_rs, t + 1)
            rows = fqk[b][:].rearrange("p c (h d) -> p (c h) d", d=FD)
            dve.tensor_tensor(rows, rows, frs[:].unsqueeze(2).to_broadcast([P, 2 * FH, FD]), ALU.mult).then_inc(f_n, 1)
            wait(dve, f_n, t + 1)
            for c in range(2):
                rows = fqk[b][:, c, :].rearrange("p (h d) -> p h d", d=FD)
                dve.tensor_tensor(rows, rows, gqk[:, c, :].unsqueeze(1).to_broadcast([P, FH, FD]), ALU.mult).then_inc(f_g, 1)
            wait(dve, ds_mm, t + 1)
            for h in range(GH):
                dve.scalar_tensor_tensor(out=S[:, h, :], in0=S[:, h, :], scalar=eb[:, h, n_last - 1:n_last], in1=ds_ps[:, h, :],
                                         op0=ALU.mult, op1=ALU.add).then_inc(s_up, 1)
            wait(dve, o_std, t + 1)
            dve.reciprocal(ors[:], ostd[:]).then_inc(o_rs, 1)
            wait(dve, o_rs, t + 1)
            wait(dve, sg, t + 1)
            for h in range(GH):
                dve.scalar_tensor_tensor(out=mixg[b][:, h * GV:(h + 1) * GV], in0=O[:, h, :], scalar=ors[:, h:h + 1],
                                         in1=zg[b][:, h * GV:(h + 1) * GV], op0=ALU.mult, op1=ALU.mult).then_inc(mixd, 1)

        def past():
            dve.wait_ge(past_mm, 1)
            dve.tensor_copy(past_sum[:], C[0:PB * FH, P - 1:P]).then_inc(past_s, 1)
            dve.wait_ge(past_c, 1)
            dve.tensor_copy(past_carry[:], C[0:PB * FH, 128:129]).then_inc(past_s, 1)
            dve.wait_ge(past_s, 2)
            dve.tensor_scalar(past_nc[:], C[0:PB * FH, 0:P], past_carry[:], -1.0, ALU.add, ALU.mult).then_inc(past_r, 1)
            dve.wait_ge(c_c, TILES + 1)
            dve.tensor_scalar(carry[:], C[0:FH, 256:257], -1.0, None, ALU.mult).then_inc(past_r, 1)
            dve.wait_ge(past_r, 2)
            dve.wait_ge(s_ld, 16)
        dve.memset(eps[:], EPS).then_inc(inited, 1)
        dve.memset(ones[:], 1.0)
        dve.memset(carry[:], 0.0).then_inc(c_c, 1)
        dve.memset(S[:], 0.0)
        for b in range(2):
            dve.memset(lq[b][:], 0.0)
            dve.memset(lk[b][:], 0.0)
        dve.memset(lev[:], 0.0).then_inc(inited, 1)
        dve.wait_ge(cst, 16 * 11)
        for k in range(KD):
            dve.wait_ge(w_ld[k], 16)
            dve.tensor_scalar(w[:, k, :], w[:, k, :], g1[:, k:k + 1], None, ALU.mult).then_inc(w_sc, 1)
        over_tiles(dve, tile, past)


def attend_phase(nc, ctx, io, dram):
    def sb(n, s, d=F32):
        return ctx.enter_context(nc.sbuf_tensor(n, s, d))

    def ps(n, s, d=F32):
        return ctx.enter_context(nc.psum_tensor(n, s, d))

    def sem(n):
        return ctx.enter_context(nc.semaphore(n))

    KA = FD + 1
    w = sb("w_out", [P, KD, D])
    ident = sb("ident_f", [P, P])
    identb = sb("ident_b", [P, P], BF16)
    causal = sb("causal_neg", [P, 2, P], BF16)
    kT = sb("k_aug_T", [KA, FH, PAST + S_T])
    qT = sb("q_aug_T", [KA, FH, P])
    qh = [sb(f"q_head{b}", [KA, P]) for b in range(2)]
    v = sb("v_rows", [P, TILES + 1, FH * FD])
    kr = [sb(f"k_rows{b}", [P, FH * FD]) for b in range(2)]
    qr = [sb(f"q_rows{b}", [P, FH * FD]) for b in range(2)]
    xr = [sb(f"x_res{b}", [P, D]) for b in range(2)]
    mix = [sb(f"mix_rows{b}", [P, D]) for b in range(2)]
    mixT = sb("mix_T", [P, KD, P])
    xm = [sb(f"x_mid{b}", [P, D]) for b in range(2)]
    m = [sb(f"row_max{b}", [P, 1]) for b in range(2)]
    nm = [sb(f"neg_max{b}", [P, 1]) for b in range(2)]
    pr = [sb(f"prob_rows{b}", [P, PAST + S_T]) for b in range(2)]
    pT = [sb(f"prob_T{b}", [P, 4, P]) for b in range(2)]
    l = sb("row_sums", [P, FH])
    rl = sb("row_sums_inv", [P, FH])

    S = [ps("ps_scores0", [P, 1536]), ps("ps_scores1", [P, 1024])]
    Q = [ps(f"ps_quad{b}", [P, 4, P]) for b in range(2)]
    O = ps("ps_fox_o", [P, FH, FD])

    cst = sem("attend_consts_loaded")
    wld = sem("w_out_loaded")
    kv_in = sem("keys_values_loaded")
    t_in = [sem(f"attend_rows_loaded{b}") for b in range(2)]
    one = sem("aug_ones_set")
    kq_t = sem("kq_quads_transposed")
    kq_ev = sem("kq_quads_ready")
    q_cp = sem("q_head_copied")
    s_mm = sem("scores_done")
    mx = sem("row_max_ready")
    nmx = sem("neg_max_ready")
    ex = sem("probs_ready")
    p_t = sem("prob_quads_transposed")
    p_ev = sem("prob_quads_ready")
    pv = sem("prob_quads_used")
    rls = sem("row_sums_inverted")
    o_n = sem("fox_out_ready")
    mx_t = sem("mix_quads_transposed")
    mx_ev = sem("mix_T_ready")
    y_mm = sem("mixed_projected")
    xm_r = sem("x_mid_ready")
    xm_st = [sem(f"x_mid_landed{b}") for b in range(2)]
    passed = sem("attend_waits_passed")

    CR = 2

    def shape(t):
        blocks = [P] * (t + 1) if t < TILES else [P] * PB + [S_T]
        total = sum(blocks)
        chunks = [(a, min(a + 512, total)) for a in range(0, total, 512)]
        return blocks, total, chunks

    def quads(t):
        return -(-len(shape(t)[0]) // 4)

    def quads_before(t):
        return sum(FH * quads(u) for u in range(t))

    block = ctx.enter_context(nc.Block())

    @block.sync
    def _(sp):
        sp.dma_start(ident[:], dram["ident"]).then_inc(cst, 16)
        sp.dma_start(identb[:], dram["ident_b"]).then_inc(cst, 16)
        sp.dma_start(causal[:], dram["causal"]).then_inc(cst, 16)
        sp.dma_start(kT[FD:KA, :, 0:T], dram["negc"][:, 0:T].rearrange("(o h) t -> o h t", o=1)).then_inc(kv_in, 16)
        sp.dma_start(v[:, 0:TILES, :], io["p_fox_v"].rearrange("(n p) c -> p n c", p=P)).then_inc(kv_in, 16)
        for t in range(ALL):
            sample = t == TILES
            rows = S_T if sample else P
            b = t % 2
            if t >= 2:
                sp.wait_ge(kq_t, 4 * (t - 1))
                sp.wait_ge(mx_t, 2 * (t - 1))
                sp.wait_ge(xm_r, 2 * (t - 1))
            k_src = io["s_fox_k"] if sample else io["p_fox_k"][t * P:(t + 1) * P, :]
            sp.dma_start(kr[b][0:rows, :], k_src).then_inc(t_in[b], 16)
            sp.dma_start(qr[b][:], dram["q"][t]).then_inc(t_in[b], 16)
            sp.dma_start(mix[b][:, 0:GH * GV], dram["mixg"][t]).then_inc(t_in[b], 16)
            sp.dma_start(xr[b][:], dram["xr"][t]).then_inc(t_in[b], 16)
            if t == 0:
                sp.dma_start(w[:], io["w_out"][0].rearrange("(k p) n -> p k n", p=P)).then_inc(wld, 16)
            if t >= 2:
                sp.dma_start(dram["xm"][t - 2], xm[b][:]).then_inc(xm_st[b], 16)
            if sample:
                sp.wait_ge(pv, quads_before(TILES) + CR)
                sp.dma_start(kT[0:FD, :, 0:PAST], dram["kT_past"]).then_inc(kv_in, 16)
                for h in range(FH):
                    sp.dma_start(kT[FD:KA, h, 0:PAST].rearrange("o (n t) -> o n t", t=P),
                                 dram["negc_past"][h:PB * FH:FH, :].rearrange("(o n) t -> o n t", o=1)).then_inc(kv_in, 16)
                sp.dma_start(kT[FD:KA, :, PAST:PAST + S_T], dram["negc"][:, T:T + S_T].rearrange("(o h) t -> o h t", o=1)).then_inc(kv_in, 16)
                sp.dma_start(v[:, 0:PB, :], io["cache_fox_v"].rearrange("(n p) c -> p n c", p=P)).then_inc(kv_in, 16)
                sp.dma_start(v[0:S_T, PB, :], io["s_fox_v"]).then_inc(kv_in, 16)
        for t in (ALL - 2, ALL - 1):
            sp.wait_ge(xm_r, 2 * (t + 1))
            sp.dma_start(dram["xm"][t], xm[t % 2][:]).then_inc(xm_st[t % 2], 16)
        for b in range(2):
            sp.wait_ge(xm_st[b], 16 * ((ALL + 1 - b) // 2))

    @block.gpsimd
    def _(pool):
        pool.sem_inc(q_cp, CR)
        pool.wait_ge(one, 1)
        for t in range(ALL):
            pool.wait_ge(kq_ev, 4 * (t + 1))
            with pool.Fori(0, FH // 2) as hp:
                for b in range(2):
                    g = FH * t + 2 * hp + b
                    pool.wait_ge(s_mm, g - 1 + CR)
                    pool.sem_inc(passed, 1)
                    pool.tensor_copy(qh[b][:], qT[:, bass.ds(2 * hp + b, 1), :].rearrange("k o t -> k (o t)")).then_inc(q_cp, 1)

    @block.scalar
    def _(act):
        def keys_queries(t):
            rows = S_T if t == TILES else P
            at = PAST if t == TILES else t * P
            for n in range(4):
                act.wait_ge(kq_t, 4 * t + n + 1)
                hs = slice(4 * (n % 2), 4 * (n % 2) + 4)
                if n < 2:
                    act.activation(kT[0:FD, hs, at:at + rows], Q[n % 2][0:FD, :, 0:rows], ACT.Copy).then_inc(kq_ev, 1)
                else:
                    act.wait_ge(q_cp, FH * t + CR)
                    act.activation(qT[0:FD, hs, :], Q[n % 2][0:FD], ACT.Copy, scale=FOX_SCALE).then_inc(kq_ev, 1)

        act.sem_inc(ex, CR)
        keys_queries(0)
        for t in range(ALL):
            total = shape(t)[1]
            wait(act, o_n, t)
            with act.Fori(0, FH // 2) as hp:
                for b in range(2):
                    g = FH * t + 2 * hp + b
                    act.wait_ge(nmx, g + 1)
                    act.wait_ge(p_t, quads_before(t) + (2 * hp + b - 1) * quads(t) + CR)
                    act.sem_inc(passed, 1)
                    src = S[0 if t == TILES else b]
                    act.activation(pr[b][:, 0:total], src[:, 0:total], ACT.Exp, bias=nm[b][:],
                                   accum_out=l[:, bass.ds(2 * hp + b, 1)]).then_inc(ex, 1)
            if t + 1 < ALL:
                keys_queries(t + 1)
            for n in range(2):
                act.wait_ge(mx_t, 2 * t + n + 1)
                wait(act, y_mm, 2 * t)
                act.activation(mixT[:, 4 * n:4 * n + 4, :], Q[n][:], ACT.Copy).then_inc(mx_ev, 1)

    @block.tensor
    def _(pe):
        def keys_queries(t):
            rows = S_T if t == TILES else P
            pe.wait_ge(t_in[t % 2], 64 * (t // 2 + 1))
            pe.wait_ge(p_ev, quads_before(t) + CR)
            wait(pe, mx_ev, 2 * (t - 1))
            for n in range(4):
                if n >= 2:
                    pe.wait_ge(kq_ev, 4 * t + n - 1)
                src, r = (kr[t % 2], rows) if n < 2 else (qr[t % 2], P)
                for h in range(4):
                    c = (4 * (n % 2) + h) * FD
                    tr = pe.transpose(Q[n % 2][0:FD, h, 0:r], src[0:r, c:c + FD], ident[0:r, 0:r])
                tr.then_inc(kq_t, 1)

        def scores(t, h, b):
            sample = t == TILES
            blocks, total, chunks = shape(t)
            g = FH * t + h
            pe.wait_ge(q_cp, g + 1 + CR)
            dst = S[0 if sample else b]
            pe.wait_ge(ex, g - (0 if sample else 1) + CR)
            pe.sem_inc(passed, 1)
            for lo, hi in chunks:
                own = hi == total
                mm = pe.matmul(dst[:, lo:hi], qh[b][:], kT[:, bass.ds(h, 1), lo:hi].rearrange("k o t -> k (o t)"), start=True, stop=not own)
            wd = blocks[-1]
            mm = pe.matmul(dst[:, total - wd:total], identb[:], causal[:, 1 if sample else 0, 0:wd], start=False, stop=True)
            mm.then_inc(s_mm, 1)

        def first_scores(t):
            pe.wait_ge(kq_ev, 4 * (t + 1))
            pe.wait_ge(kv_in, 32 if t < TILES else 32 + 16 * (FH + 4))
            pe.wait_ge(one, 1)
            scores(t, 0, 0)

        def values(t, h, b):
            blocks = shape(t)[0]
            nq = quads(t)
            first = quads_before(t) + h * nq
            pe.wait_ge(ex, FH * t + h + 1 + CR)
            pe.sem_inc(passed, 1)

            def turn(q):
                e = (b * nq + q) % 2
                pe.wait_ge(p_ev, first + q - 1 + CR)
                pe.sem_inc(passed, 1)
                for n in range(4 * q, min(4 * q + 4, len(blocks))):
                    tr = pe.transpose(Q[e][0:blocks[n], n - 4 * q, :], pr[b][:, n * P:n * P + blocks[n]], ident[:])
                tr.then_inc(p_t, 1)

            def use(q):
                e = (b * nq + q) % 2
                pe.wait_ge(p_ev, first + q + 1 + CR)
                pe.sem_inc(passed, 1)
                for n in range(4 * q, min(4 * q + 4, len(blocks))):
                    mm = pe.matmul(O[:, bass.ds(h, 1), :].rearrange("p o d -> p (o d)"), pT[e][0:blocks[n], n - 4 * q, :],
                                   v[0:blocks[n], n, bass.ts(h, FD)], start=(n == 0), stop=(n == len(blocks) - 1))
                mm.then_inc(pv, 1)
            turn(0)
            for q in range(nq):
                if q + 1 < nq:
                    turn(q + 1)
                use(q)

        pe.sem_inc(s_mm, CR)
        pe.sem_inc(p_t, CR)
        pe.sem_inc(pv, CR)
        pe.wait_ge(cst, 48)
        keys_queries(0)
        first_scores(0)
        for t in range(ALL):
            wait(pe, xm_r, 2 * t)
            wait(pe, o_n, t)
            with pe.Fori(0, FH // 2 - 1) as hp:
                scores(t, 2 * hp + 1, 1)
                values(t, 2 * hp, 0)
                scores(t, 2 * hp + 2, 0)
                values(t, 2 * hp + 1, 1)
            scores(t, FH - 1, 1)
            values(t, FH - 2, 0)
            values(t, FH - 1, 1)
            if t + 1 < ALL:
                keys_queries(t + 1)
                pe.wait_ge(kq_ev, 4 * (t + 2))
            else:
                pe.wait_ge(p_ev, quads_before(ALL) + CR)
                pe.wait_ge(t_in[t % 2], 64 * (t // 2 + 1))
            pe.wait_ge(o_n, t + 1)
            for n in range(2):
                for k in range(4):
                    tr = pe.transpose(Q[n][:, k, :], mix[t % 2][:, (4 * n + k) * P:(4 * n + k + 1) * P], ident[:])
                tr.then_inc(mx_t, 1)
            if t + 1 < TILES:
                first_scores(t + 1)
            pe.wait_ge(mx_ev, 2 * t + 2)
            pe.wait_ge(wld, 16)
            pe.wait_ge(ex, FH * (t + 1) + CR)
            for n in range(2):
                for k in range(KD):
                    mm = pe.matmul(S[1][:, n * 512:(n + 1) * 512], mixT[:, k, :], w[:, k, n * 512:(n + 1) * 512], start=(k == 0), stop=(k == KD - 1))
                mm.then_inc(y_mm, 1)
            if t + 1 == TILES:
                first_scores(t + 1)

    @block.vector
    def _(dve):
        def row_max(t, h, b):
            g = FH * t + h
            dve.wait_ge(s_mm, g + 1 + CR)
            dve.tensor_reduce(m[b][:], S[0 if t == TILES else b][:, 0:shape(t)[1]], AX.X, ALU.max).then_inc(mx, 1)
            dve.wait_ge(mx, g + 1)
            dve.wait_ge(ex, g - 1 + CR)
            dve.tensor_scalar(nm[b][:], m[b][:], -1.0, None, ALU.mult).then_inc(nmx, 1)

        def move_quads(t, h, b):
            blocks = shape(t)[0]
            nq = quads(t)
            for q in range(nq):
                e = (b * nq + q) % 2
                n = quads_before(t) + h * nq + q
                dve.wait_ge(p_t, n + 1 + CR)
                dve.wait_ge(pv, n - 1 + CR)
                full = [x for x in blocks[4 * q:4 * q + 4] if x == P]
                if full:
                    dve.tensor_copy(pT[e][:, 0:len(full), :], Q[e][:, 0:len(full), :]).then_inc(p_ev, 1)
                else:
                    dve.tensor_copy(pT[e][0:S_T, 0, :], Q[e][0:S_T, 0, :]).then_inc(p_ev, 1)

        dve.memset(qT[FD:KA, :, :], 1.0).then_inc(one, 1)
        dve.sem_inc(p_ev, CR)
        row_max(0, 0, 0)
        for t in range(ALL):
            with dve.Fori(0, FH // 2 - 1) as hp:
                row_max(t, 2 * hp + 1, 1)
                move_quads(t, 2 * hp, 0)
                row_max(t, 2 * hp + 2, 0)
                move_quads(t, 2 * hp + 1, 1)
            row_max(t, FH - 1, 1)
            move_quads(t, FH - 2, 0)
            move_quads(t, FH - 1, 1)
            dve.wait_ge(ex, FH * (t + 1) + CR)
            dve.reciprocal(rl[:], l[:]).then_inc(rls, 1)
            dve.wait_ge(rls, t + 1)
            dve.wait_ge(pv, quads_before(t + 1) + CR)
            wait(dve, mx_t, 2 * (t - 1))
            dve.wait_ge(t_in[t % 2], 64 * (t // 2 + 1))
            dve.tensor_tensor(mix[t % 2][:, GH * GV:].rearrange("p (h d) -> p h d", d=FD), O[:],
                              rl[:].unsqueeze(2).to_broadcast([P, FH, FD]), ALU.mult).then_inc(o_n, 1)
            if t + 1 < TILES:
                row_max(t + 1, 0, 0)
            for n in range(2):
                dve.wait_ge(y_mm, 2 * t + 2)
                wait(dve, xm_st[t % 2], 16 * (t // 2))
                dve.tensor_tensor(xm[t % 2][:, n * 512:(n + 1) * 512], S[1][:, n * 512:(n + 1) * 512], xr[t % 2][:, n * 512:(n + 1) * 512], ALU.add).then_inc(xm_r, 1)
            if t + 1 == TILES:
                row_max(t + 1, 0, 0)


def peer_phase(nc, ctx, io, dram):
    def sb(n, s, d=F32):
        return ctx.enter_context(nc.sbuf_tensor(n, s, d))

    def ps(n, s, d=F32):
        return ctx.enter_context(nc.psum_tensor(n, s, d))

    def sem(n):
        return ctx.enter_context(nc.semaphore(n))

    RING = 8
    STEP = 2 * RING
    GRP = 4
    K2 = TOPK * TOPK
    w = sb("w_peer_q", [P, KD, PH * 2 * DKEY])
    sub = sb("subkeys_T", [P, PH * 2, NKEY])
    g2 = sb("g_norm2_rows", [P, D])
    ident = sb("ident_p", [P, P])
    fold = sb("fold_copies", [P, P])
    iota = sb("iota16", [P, TOPK])
    eps = sb("eps_peer", [P, 1])
    xm = [sb(f"x_mid_in{b}", [P, D]) for b in range(2)]
    h2 = [sb(f"h2_rows{b}", [P, D]) for b in range(2)]
    h2T = sb("h2_T", [P, KD, P])
    hss = sb("h2_sumsq", [P, 1])
    hstd = sb("h2_std", [P, 1])
    hrs = sb("h2_rstd", [P, 1])
    qr = sb("peer_q_rows", [P, 2 * DKEY])
    qT = sb("peer_q_T", [P, 2, P])
    s1 = sb("key_scores", [P, 2, NKEY])
    s2 = sb("key_scores_rest", [P, 2, NKEY])
    kv = sb("key_top", [P, 2, TOPK])
    ki = sb("key_top_index", [P, 2, TOPK], U32)
    kf = sb("key_top_index_f", [P, 2, TOPK])
    cand = sb("candidates", [P, TOPK, TOPK])
    cand2 = sb("candidates_rest", [P, TOPK, TOPK])
    tv = sb("expert_top", [P, TOPK])
    ti = sb("expert_top_index", [P, TOPK], U32)
    ab = sb("expert_pair", [P, 2, TOPK], U32)
    hot = sb("expert_pair_one_hot", [P, 2, TOPK, TOPK])
    pick = sb("expert_pair_keys", [P, 2, TOPK])
    nmx = sb("neg_top", [P, 1])
    pe_ = sb("top_exp", [P, TOPK])
    psum_ = sb("top_exp_sum", [P, 1])
    pinv = sb("top_exp_sum_inv", [P, 1])
    idx = [sb(f"expert_index{b}", [P, SLOTS], U32) for b in range(2)]
    gw = [sb(f"expert_weight{b}", [P, SLOTS]) for b in range(2)]
    idx_s = sb("sample_index", [P, SLOTS // COPIES], U32)
    gw_s = sb("sample_weight", [P, SLOTS // COPIES])
    ixs = sb("staged_index", [P, 2, RING], U32)
    ring = sb("uv_ring", [P, RING, 2 * D])
    dots = sb("u_dot_h", [P, 2, GRP])
    gel = sb("gelu_u_dot_h", [P, 2, GRP])
    coef = sb("coefficients", [P, 2, GRP])
    diag = sb("coef_diag", [P, RING, P])
    sums = [sb(f"v_sums{b}", [P, D]) for b in range(2)]
    res = sb("y_rows", [P, D])

    acc = [ps(f"ps_acc{b}", [P, 2, 512]) for b in range(2)]
    TB = [ps(f"ps_turn{b}", [P, 4, P]) for b in range(2)]
    QR = ps("ps_q_rows", [P, 512])
    SC = ps("ps_key_scores", [P, 512])

    cst = sem("peer_consts_loaded")
    wld = [sem(f"peer_weights_loaded{b}") for b in range(2)]
    sub_in = sem("subkeys_loaded")
    init = sem("peer_inited")
    x_in = [sem(f"x_mid_loaded{b}") for b in range(2)]
    p_sq = sem("h2_squared")
    p_std = sem("h2_std_ready")
    p_rs = sem("h2_rstd_ready")
    p_h2 = sem("h2_ready")
    p_t = sem("h2_transposed")
    p_ev = sem("h2_T_ready")
    q_mm = sem("peer_q_done")
    q_ev = sem("peer_q_rows_ready")
    qt_t = sem("peer_q_transposed")
    qt_ev = sem("peer_q_T_ready")
    s_mm = sem("key_scores_done")
    s_ev = sem("key_scores_ready")
    chain = sem("routing_steps")
    ex = sem("top_exp_ready")
    nmr = sem("neg_top_ready")
    routed = sem("head_routed")
    spread = sem("sample_slots_spread")
    staged = sem("index_staged")
    slot = [sem(f"uv_landed{r}") for r in range(RING)]
    dotted = sem("u_dotted")
    geld = sem("gelu_ready")
    cfd = sem("coefficients_ready")
    dgd = sem("diagonal_ready")
    summed = sem("v_summed")
    a_in = sem("acc_started")
    a_ev = sem("y_rows_ready")
    y_st = sem("y_landed")
    added = sem("v_added")
    cleared = sem("sums_cleared")
    spread_w = sem("sample_weights_spread")
    passed = sem("peer_waits_passed")
    CR = 2

    block = ctx.enter_context(nc.Block())

    def pipeline(eng, pre, open_, step, finish):
        def first_heads(t, b):
            open_(t, b)
            with eng.Fori(0, (PH - LAG) // HEADS_PER_LOOP) as i:
                for n in range(HEADS_PER_LOOP):
                    j = HEADS_PER_LOOP * i + n
                    step(t, b, j, (t, b, j + LAG))

        def last_heads(t, b, u):
            pre(t + 1, 1 - b, u)
            for j in range(LAG):
                step(t, b, PH - LAG + j, (t + 1, 1 - b, j))

        pre(0, 0, 1)
        for j in range(LAG):
            step(None, 0, 0, (0, 0, j))
        first_heads(0, 0)
        last_heads(0, 0, 1)
        first_heads(1, 1)
        finish(0, 0)
        with eng.Fori(0, TILES // 2 - 1) as i:
            for b in range(2):
                t = 2 * i + 1 + b
                last_heads(t, 1 - b, i + 2)
                first_heads(t + 1, b)
                finish(t, 1 - b)
        last_heads(TILES - 1, 1, TILES // 2 + 1)
        open_(TILES, 0)
        for j in range(PH):
            step(TILES, 0, j, (TILES, 0, j + LAG) if j + LAG < PH else None)
            if j == PH // 2:
                finish(TILES - 1, 1)
        finish(TILES, 0)

    LAG = 2
    HEADS_PER_LOOP = 3

    def nothing(*_):
        pass

    PT = RING - 2
    DONE = PT * (SLOTS // RING) * TILES
    ADDED = 2 * (SLOTS // RING) * TILES

    def place(r):
        return r - r // GRP

    def summed_of(t, j, c, r):
        return PT * ((SLOTS // RING) * t + 2 * j + c) + place(r) + 1

    def added_of(t, j, c, r):
        return 2 * ((SLOTS // RING) * t + 2 * j + c - 1) + r // GRP + 1 + CR

    def free_of_sample(eng, j, n):
        r = GRP * (j % 2) + n
        if j >= 2:
            eng.wait_ge(summed, DONE + PT + GRP * (j - 2) + n + 1)
        elif n < GRP - 1:
            eng.wait_ge(summed, DONE + place(r) + 1)
        else:
            eng.wait_ge(added, ADDED - 2 + r // GRP + 1 + CR)

    def group(t, j, q=0):
        return (SLOTS // GRP) * t + (j if t is TILES else (STEP // GRP) * j + q)

    @block.sync
    def _(sp):
        for dst, src in ((ident[:], dram["ident"]), (g2[:], io["g_norm2"].to_broadcast([P, D])),
                         (fold[:], dram["fold"]), (iota[:], dram["iota"])):
            sp.dma_start(dst, src).then_inc(cst, 16)

        def weights(n, cols):
            sp.dma_start(w[:, :, cols], io["w_peer_q"][0][:, cols].rearrange("(k p) n -> p k n", p=P)).then_inc(wld[n], 16)
        weights(0, slice(0, LAG * 2 * DKEY))
        sp.dma_start(sub[:], dram["subkeys_T"]).then_inc(sub_in, 16)
        weights(1, slice(LAG * 2 * DKEY, PH * 2 * DKEY))

    @block.gpsimd
    def _(pool):
        def gather(r, index):
            pool.indirect_dma_start(out=ring[:, r, :], out_offset=None, in_=dram["uv"],
                                    in_offset=bass.IndirectOffsetOnAxis(ap=index, axis=0)).then_inc(slot[r], 16)

        def load(t, b):
            pool.dma_start(xm[b][:], dram["xm"][bass.ds(t, 1)].rearrange("o p n -> (o p) n")).then_inc(x_in[b], 16)

        def open_(t, b):
            if t is TILES:
                return
            pool.wait_ge(a_in, t + CR)
            pool.wait_ge(p_h2, t + 1)
            pool.sem_inc(passed, 1)
            load(t + 1, 1 - b)

        def stage(t, b, j, c):
            pool.wait_ge(routed, PH * t + j + 1 + CR)
            pool.sem_inc(passed, 1)
            pool.tensor_copy(ixs[:, c, :], idx[b][:, bass.ds(STEP * j + RING * c, RING)]).then_inc(staged, 1)

        def step(t, b, j, route):
            if t is None:
                if route[2] == 0:
                    stage(0, 0, 0, 0)
                return
            if t is TILES:
                pool.wait_ge(spread, COPIES * (j + 1))
                for n in range(GRP):
                    free_of_sample(pool, j, n)
                    gather(GRP * (j % 2) + n, idx_s[:, GRP * j + n:GRP * j + n + 1])
                return
            for c in range(2):
                pool.wait_ge(staged, 2 * PH * t + 2 * j + c + 1)
                for r in range(RING):
                    if r % GRP < GRP - 1:
                        pool.wait_ge(summed, summed_of(t, j, c, r))
                    else:
                        pool.wait_ge(added, added_of(t, j, c, r))
                    pool.sem_inc(passed, 1)
                    if r == RING - 1:
                        if c == 0:
                            stage(t, b, j, 1)
                        elif not isinstance(j, int) or j < PH - 1:
                            stage(t, b, j + 1, 0)
                        elif not isinstance(t, int) or t < TILES - 1:
                            stage(t + 1, 1 - b, 0, 0)
                    gather(r, ixs[:, c, r:r + 1])
        load(0, 0)
        pool.wait_ge(init, 2)
        pipeline(pool, nothing, open_, step, nothing)

    @block.scalar
    def _(act):
        for given, n in ((q_ev, CR), (qt_ev, CR), (s_ev, CR), (p_ev, CR), (geld, CR), (dgd, PT)):
            act.sem_inc(given, n)
        act.wait_ge(cst, 64)
        act.wait_ge(init, 2)

        def squares(t, b, u):
            act.wait_ge(x_in[b], 16 * u)
            act.wait_ge(dotted, SLOTS * (t - 1) + 1 if not isinstance(t, int) or t else 1)
            act.activation(h2[b][:], xm[b][:], ACT.Square, accum_out=hss[:]).then_inc(p_sq, 1)
            act.wait_ge(p_sq, t + 1)
            act.activation(hstd[:], hss[:], ACT.Sqrt, bias=eps[:], scale=1.0 / D).then_inc(p_std, 1)

        def pre(t, b, u):
            squares(t, b, u)
            act.wait_ge(q_mm, PH * t + CR)
            for n in range(2):
                act.wait_ge(p_t, 2 * t + n + 1)
                act.activation(h2T[:, 4 * n:4 * n + 4, :], TB[n][:], ACT.Copy).then_inc(p_ev, 1)

        def route_part(n, part):
            if part == 0:
                act.wait_ge(q_mm, n + 1 + CR)
                act.wait_ge(qt_t, n + CR)
                act.activation(qr[:], QR[:, 0:2 * DKEY], ACT.Copy).then_inc(q_ev, 1)
            if part == 1:
                act.wait_ge(qt_t, n + 1 + CR)
                act.wait_ge(s_mm, n + CR)
                act.activation(qT[:], TB[0][:, 0:2, :], ACT.Copy).then_inc(qt_ev, 1)
            if part == 2:
                act.wait_ge(s_mm, n + 1 + CR)
                act.wait_ge(routed, n + CR)
                act.activation(s1[:], SC[:, 0:2 * NKEY].rearrange("p (c k) -> p c k", c=2), ACT.Copy).then_inc(s_ev, 1)
            if part == 3:
                act.wait_ge(nmr, n + 1)
                act.activation(pe_[:], tv[:], ACT.Exp, bias=nmx[:], accum_out=psum_[:]).then_inc(ex, 1)

        def slots(t, j, q):
            g = group(t, j, q)
            act.wait_ge(dotted, GRP * (g + 1) + 1)
            act.wait_ge(cfd, g - 1 + CR)
            act.activation(gel[:, q % 2, :], dots[:, q % 2, :], ACT.Gelu).then_inc(geld, 1)
            act.wait_ge(cfd, g + 1 + CR)
            for n in range(GRP if t is TILES else GRP - 1):
                r = (GRP * q + n) % RING
                if t is TILES:
                    if n == GRP - 1 and j < 2:
                        pass
                    else:
                        free_of_sample(act, j, n)
                else:
                    act.wait_ge(summed, summed_of(t, j, q // 2, r))
                matrix = fold if t is TILES else ident
                act.activation(diag[:, r, :], matrix[:], ACT.Copy, scale=coef[:, q % 2, n:n + 1]).then_inc(dgd, 1)

        def step(t, b, j, route):
            n = None if route is None else PH * route[0] + route[2]
            if t is None or t is TILES:
                if n is not None:
                    for part in range(3):
                        route_part(n, part)
                if t is TILES:
                    slots(t, j, j % 2)
                if n is not None:
                    route_part(n, 3)
                return
            route_part(n, 0)
            slots(t, j, 0)
            route_part(n, 1)
            route_part(n, 2)
            slots(t, j, 1)
            slots(t, j, 2)
            route_part(n, 3)
            slots(t, j, 3)

        def finish(t, b):
            act.wait_ge(a_ev, 2 * t + 2 + 2 * CR)
            if t is TILES:
                act.dma_start(io["y_s"], res[0:S_T, :]).then_inc(y_st, 16)
            else:
                act.dma_start(io["y_p"][bass.ts(t, P), :], res[:]).then_inc(y_st, 16)
        pipeline(act, pre, nothing, step, finish)
        act.wait_ge(y_st, 16 * ALL)

    @block.tensor
    def _(pe):
        for given, n in ((summed, PT), (q_mm, CR), (qt_t, CR), (s_mm, CR), (a_in, CR)):
            pe.sem_inc(given, n)
        pe.wait_ge(cst, 64)
        pe.wait_ge(wld[0], 16)

        def pre(t, b, u):
            pe.wait_ge(p_h2, t + 1)
            pe.wait_ge(qt_ev, PH * t + CR)
            pe.wait_ge(p_ev, 2 * t + CR)
            pe.sem_inc(passed, 1)
            for n in range(2):
                for k in range(4):
                    tr = pe.transpose(TB[n][:, k, :], h2[b][:, (4 * n + k) * P:(4 * n + k + 1) * P], ident[:])
                tr.then_inc(p_t, 1)

        def route_part(route, part):
            if route is None:
                return
            t, _, j = route
            n = PH * t + j
            if part == 0:
                pe.wait_ge(q_ev, n + CR)
                pe.wait_ge(p_ev, 2 * t + 2 + CR)
                pe.sem_inc(passed, 1)
                for k in range(KD):
                    mm = pe.matmul(QR[:, 0:2 * DKEY], h2T[:, k, :], w[:, k, bass.ts(j, 2 * DKEY)], start=(k == 0), stop=(k == KD - 1))
                mm.then_inc(q_mm, 1)
            if part == 1:
                pe.wait_ge(q_ev, n + 1 + CR)
                pe.wait_ge(qt_ev, n + CR)
                pe.sem_inc(passed, 1)
                for c in range(2):
                    tr = pe.transpose(TB[0][:, c, :], qr[:, c * DKEY:(c + 1) * DKEY], ident[:])
                tr.then_inc(qt_t, 1)
            if part == 2:
                pe.wait_ge(qt_ev, n + 1 + CR)
                pe.wait_ge(s_ev, n + CR)
                pe.sem_inc(passed, 1)
                if isinstance(n, int) and n == 0:
                    pe.wait_ge(sub_in, 16)
                for c in range(2):
                    mm = pe.matmul(SC[:, c * NKEY:(c + 1) * NKEY], qT[:, c, :], sub[:, bass.ds(2 * j + c, 1), :].rearrange("p o k -> p (o k)"),
                                   start=True, stop=True)
                mm.then_inc(s_mm, 1)

        def open_(t, b):
            if isinstance(t, int) and t == 0:
                pe.wait_ge(wld[1], 16)
            pe.wait_ge(a_ev, 2 * (t - 1) + 2 * CR)
            for n in range(2):
                mm = pe.matmul(acc[b][:, n, :], ident[:], xm[b][:, n * 512:(n + 1) * 512], start=True, stop=False, skip_group_check=True)
            mm.then_inc(a_in, 1)

        def add(b, r):
            for c in range(2):
                mm = pe.matmul(acc[b][:, c, :], diag[:, r, :], ring[:, r, D + c * 512:D + (c + 1) * 512], start=False, stop=False, skip_group_check=True)
            mm.then_inc(summed, 1)

        def step(t, b, j, route):
            if t is None or t is TILES:
                for part in range(3):
                    route_part(route, part)
                if t is TILES:
                    for n in range(GRP):
                        pe.wait_ge(dgd, DONE + PT + GRP * j + n + 1)
                        add(b, GRP * (j % 2) + n)
                return
            route_part(route, 0)
            for q in range(STEP // GRP):
                for n in range(GRP - 1):
                    r = (GRP * q + n) % RING
                    pe.wait_ge(dgd, summed_of(t, j, q // 2, r) + PT)
                    add(b, r)
                    if q == 0 and n == 1:
                        route_part(route, 1)
                if q == 0:
                    route_part(route, 2)
        pipeline(pe, pre, open_, step, nothing)

    @block.vector
    def _(dve):
        dve.memset(eps[:], EPS).then_inc(init, 1)
        dve.memset(cand2[:], 0.0).then_inc(init, 1)
        for given, n in ((dotted, 1), (cfd, CR), (routed, CR), (added, CR), (a_ev, 2 * CR)):
            dve.sem_inc(given, n)
        dve.wait_ge(cst, 64)
        STEPS = 25

        def rows(t, b):
            dve.wait_ge(p_std, t + 1)
            dve.reciprocal(hrs[:], hstd[:]).then_inc(p_rs, 1)
            dve.wait_ge(p_rs, t + 1)
            dve.scalar_tensor_tensor(out=h2[b][:], in0=xm[b][:], scalar=hrs[:], in1=g2[:], op0=ALU.mult, op1=ALU.mult).then_inc(p_h2, 1)

        def pre(t, b, u):
            rows(t, b)

        def open_(t, b):
            if t is TILES:
                return
            dve.wait_ge(a_ev, 2 * (t - 1) + 2 * CR)
            dve.memset(sums[b][:], 0.0).then_inc(cleared, 1)
            dve.wait_ge(cleared, t + 1)
            dve.sem_inc(passed, 1)

        def router(t, rb, j):
            n = PH * t + j
            done = [0]

            def ready():
                dve.wait_ge(chain, STEPS * n + done[0])
                dve.sem_inc(passed, 1)

            def did(ins):
                done[0] += 1
                ins.then_inc(chain, 1)

            def top16(values, rest, v, i, count):
                for c in range(count):
                    did(dve.max(out=v(c)[:, 0:8], in_=values(c)))
                yield
                ready()
                for c in range(count):
                    did(dve.max_index(out=i(c)[:, 0:8], in_max=v(c)[:, 0:8], in_values=values(c)))
                    did(dve.match_replace(out=rest(c), in_to_replace=v(c)[:, 0:8], in_values=values(c), imm_value=NEG_FILL))
                yield
                ready()
                for c in range(count):
                    did(dve.max(out=v(c)[:, 8:16], in_=rest(c)))
                yield
                ready()
                for c in range(count):
                    did(dve.max_index(out=i(c)[:, 8:16], in_max=v(c)[:, 8:16], in_values=rest(c)))

            dve.wait_ge(s_ev, n + 1 + CR)
            dve.sem_inc(passed, 1)
            yield from top16(lambda c: s1[:, c, :], lambda c: s2[:, c, :], lambda c: kv[:, c, :], lambda c: ki[:, c, :], 2)
            yield
            ready()
            did(dve.tensor_tensor(cand[:], kv[:, 0, :].unsqueeze(2).to_broadcast([P, TOPK, TOPK]),
                                  kv[:, 1, :].unsqueeze(1).to_broadcast([P, TOPK, TOPK]), ALU.add))
            did(dve.tensor_copy(kf[:], ki[:]))
            yield
            ready()
            flat = cand[:].rearrange("p a b -> p (a b)")
            flat2 = cand2[:].rearrange("p a b -> p (a b)")
            yield from top16(lambda c: flat, lambda c: flat2, lambda c: tv[:], lambda c: ti[:], 1)
            dve.tensor_scalar(nmx[:], tv[:, 0:1], -1.0, None, ALU.mult).then_inc(nmr, 1)
            yield
            ready()
            did(dve.tensor_scalar(ab[:, 0, :], ti[:], 4, None, ALU.logical_shift_right))
            did(dve.tensor_scalar(ab[:, 1, :], ti[:], TOPK - 1, None, ALU.bitwise_and))
            yield
            ready()
            did(dve.tensor_tensor(hot[:], ab[:].unsqueeze(3).to_broadcast([P, 2, TOPK, TOPK]),
                                  iota[:].unsqueeze(1).unsqueeze(1).to_broadcast([P, 2, TOPK, TOPK]), ALU.is_equal))
            yield
            ready()
            did(dve.tensor_tensor(hot[:], hot[:], kf[:].unsqueeze(2).to_broadcast([P, 2, TOPK, TOPK]), ALU.mult))
            dve.wait_ge(ex, n + 1)
            did(dve.reciprocal(pinv[:], psum_[:]))
            yield
            ready()
            did(dve.tensor_reduce(pick[:], hot[:], AX.X, ALU.add))
            did(dve.tensor_scalar(gw[rb][:, bass.ts(j, TOPK)], pe_[:], pinv[:], None, ALU.mult))
            yield
            ready()
            did(dve.scalar_tensor_tensor(out=idx[rb][:, bass.ts(j, TOPK)], in0=pick[:, 0, :], scalar=float(NKEY), in1=pick[:, 1, :],
                                         op0=ALU.mult, op1=ALU.add))
            assert done[0] == STEPS, done
            ready()
            dve.sem_inc(routed, 1)

        def dot(t, b, j, q, piece, first):
            dve.wait_ge(geld, group(t, j, q) - 1 + CR)
            for n in range(GRP):
                r = (GRP * q + n) % RING
                uses = (SLOTS // RING) * t + (j // 2 if t is TILES else 2 * j + q // 2) + 1
                dve.wait_ge(slot[r], 16 * uses)
                dve.tensor_tensor_reduce(out=ring[:, r, 0:D], in0=ring[:, r, 0:D], in1=h2[b][:], scale=1.0, scalar=0.0,
                                         op0=ALU.mult, op1=ALU.add, accum_out=dots[:, q % 2, n:n + 1]).then_inc(dotted, 1)
                if GRP * q + n >= first:
                    piece()

        def weigh(t, b, j, q):
            g = group(t, j, q)
            dve.wait_ge(geld, g + 1 + CR)
            if t is TILES:
                dve.wait_ge(dgd, DONE + PT + GRP * (j - 1) if j else DONE + PT - 3)
                dve.tensor_tensor(coef[:, q % 2, :], gel[:, q % 2, :], gw_s[:, GRP * j:GRP * j + GRP], ALU.mult).then_inc(cfd, 1)
                return
            dve.wait_ge(dgd, 3 * (g - 1) + PT)
            dve.wait_ge(added, g - 1 + CR)
            dve.tensor_tensor(coef[:, q % 2, :], gel[:, q % 2, :], gw[b][:, bass.ds(STEP * j + GRP * q, GRP)], ALU.mult).then_inc(cfd, 1)
            dve.wait_ge(cfd, g + 1 + CR)
            dve.wait_ge(added, g + CR)
            r = (GRP * q + GRP - 1) % RING
            dve.scalar_tensor_tensor(out=sums[b][:], in0=ring[:, r, D:], scalar=coef[:, q % 2, GRP - 1:GRP], in1=sums[b][:],
                                     op0=ALU.mult, op1=ALU.add).then_inc(added, 1)

        def spread_slots(b, h):
            for dst, src, signal in ((idx_s, idx[b], spread), (gw_s, gw[b], spread_w)):
                for c in range(COPIES):
                    p = slice(c * S_T, (c + 1) * S_T)
                    o = TOPK * h + GRP * c
                    dve.tensor_copy(dst[p, GRP * h:GRP * h + GRP], src[p, o:o + GRP]).then_inc(signal, 1)

        def step(t, b, j, route):
            pieces = router(*route) if route else iter(())

            def piece():
                next(pieces, None)
            if t is TILES:
                for h in range(0 if j == 0 else j + 1, min(j + 2, PH)):
                    spread_slots(b, h)
                dve.wait_ge(spread_w, COPIES * (j + 1))
                dot(t, b, j, j % 2, piece, 0)
                piece()
                weigh(t, b, j, j % 2)
            elif t is not None:
                for q in range(STEP // GRP):
                    dot(t, b, j, q, piece, 6)
                    if q:
                        piece()
                    weigh(t, b, j, q)
            for _ in pieces:
                pass

        def finish(t, b):
            if not isinstance(t, int) or t > 0:
                dve.wait_ge(y_st, 16 * t)
                dve.sem_inc(passed, 1)
            dve.wait_ge(summed, DONE + PT + GRP * PH if t is TILES else PT * (SLOTS // RING) * (t + 1) + PT)
            if t is not TILES:
                dve.wait_ge(added, (SLOTS // GRP) * (t + 1) + CR)
            for n in range(2):
                half = slice(n * 512, (n + 1) * 512)
                if t is TILES:
                    ins = dve.tensor_copy(res[:, half], acc[b][:, n, :])
                else:
                    ins = dve.tensor_tensor(res[:, half], acc[b][:, n, :], sums[b][:, half], ALU.add)
                ins.then_inc(a_ev, 1)
        pipeline(dve, pre, open_, step, finish)


def program(nc, io, dram):
    with ExitStack() as ctx:
        mix_phase(nc, ctx, io, dram)
    with ExitStack() as ctx:
        attend_phase(nc, ctx, io, dram)
    with ExitStack() as ctx:
        peer_phase(nc, ctx, io, dram)


_WEIGHTS = ["g_norm1", "w_in", "w_gla_a2", "b_gla_a", "g_gla_onorm", "g_fox_qnorm", "g_fox_knorm", "b_fox_f",
            "w_out", "g_norm2", "w_peer_q"]


def kernel(**inputs):
    import numpy as np
    import concourse.bacc as bacc
    from concourse.bass_utils import run_bass_kernel_spmd

    nc = bacc.Bacc("TRN2", target_bir_lowering=False, num_devices=1)
    arrays = {}

    def inp(name, a):
        a = np.ascontiguousarray(a)
        arrays["in_" + name] = a
        return nc.dram_tensor("in_" + name, a.shape, mybir.dt.from_np(a.dtype), kind="ExternalInput").ap()

    def out(name, shape):
        return nc.dram_tensor("out_" + name, shape, F32, kind="ExternalOutput").ap()

    x = {k: np.asarray(v) for k, v in inputs.items()}
    io = {name: inp(name, x[name]) for name in _WEIGHTS}
    io["cache_fox_logf"] = inp("cache_fox_logf", x["cache_fox_logf"])
    io["state_gla"] = inp("state_gla", x["state_gla"][0, 0])
    for s, n in (("p", T), ("s", S_T)):
        io[s + "_fox_k"] = out(s + "_fox_k", (n, FH * FD))
        io[s + "_fox_v"] = out(s + "_fox_v", (n, FH * FD))
        io[s + "_fox_logf"] = out(s + "_fox_logf", (n, FH))
        io[s + "_state"] = out(s + "_state", (GH, GK, GV))
        io["y_" + s] = out("y_" + s, (n, D))

    rows = np.concatenate([x["x_prompt"][0]] + [x["x_sample"][0]] * COPIES).reshape(ALL, P, D)
    dram = {
        "xr": inp("x_rows", rows),
        "xT": inp("x_T", rows.reshape(ALL, P, KD, P).transpose(0, 3, 2, 1).reshape(ALL, P, D)),
    }
    dram["uv"] = inp("peer_uv", np.concatenate([x["peer_u"][0], x["peer_v"][0]], axis=1))
    dram["subkeys_T"] = inp("subkeys_T", x["peer_subkeys"][0].transpose(3, 0, 1, 2).reshape(P, PH * 2, NKEY))
    dram["iota"] = inp("iota16", np.tile(np.arange(TOPK, dtype=np.float32), (P, 1)))
    dram["fold"] = inp("fold_copies", (np.arange(P)[:, None] % S_T == np.arange(P)[None, :] % S_T).astype(np.float32))
    dram["g1"] = inp("g_norm1_T", x["g_norm1"].reshape(KD, P).T)
    s, t = np.arange(P)[:, None], np.arange(P)[None, :]
    tri = np.stack([s <= t, (s <= t) & (s // S_T == t // S_T)], axis=1)
    level = [(s // (2 * h) == t // (2 * h)) & (s % (2 * h) < h) & (t % (2 * h) >= h) for h in LEVELS] + [s == t]
    n, m = np.arange(PB * FH)[:, None], np.arange(PB * FH)[None, :]
    before = (n % FH == m % FH) & (n // FH < m // FH)
    dram["ident"] = inp("ident", np.eye(P, dtype=np.float32))
    dram["tri"] = inp("tri", tri.astype(np.float32))
    dram["masks"] = inp("level_masks", np.stack(level, axis=1).astype(np.uint32))
    dram["earlier"] = inp("earlier_blocks", np.concatenate([before, n % FH == np.arange(FH)[None, :]], axis=1).astype(np.float32))
    import ml_dtypes
    dram["ident_b"] = inp("ident_bf16", np.eye(P, dtype=ml_dtypes.bfloat16))
    dram["causal"] = inp("causal_neg", (np.stack([t > s, t > s % S_T], axis=1) * NEG).astype(ml_dtypes.bfloat16))
    dram["kT_past"] = inp("past_k_T", x["cache_fox_k"][0, 0].transpose(2, 1, 0))
    io["cache_fox_v"] = inp("cache_fox_v", x["cache_fox_v"].reshape(PAST, FH * FD))
    for name, shape in (("xm", (ALL, P, D)), ("q", (ALL, P, FH * FD)), ("mixg", (ALL, P, GH * GV)), ("negc", (FH, ALL * P)), ("negc_past", (PB * FH, P))):
        dram[name] = nc.dram_tensor("scratch_" + name, shape, F32).ap()
    program(nc, io, dram)
    r = run_bass_kernel_spmd(nc, [arrays], core_ids=[0]).results[0]

    def got(name, *shape):
        return r["out_" + name].reshape(shape)

    return (got("y_p", 1, T, D), got("y_s", 1, S_T, D),
            got("p_fox_k", 1, 1, T, FH, FD), got("p_fox_v", 1, 1, T, FH, FD), got("p_fox_logf", 1, 1, T, FH),
            got("p_state", 1, 1, GH, GK, GV),
            got("s_fox_k", 1, 1, S_T, FH, FD), got("s_fox_v", 1, 1, S_T, FH, FD), got("s_fox_logf", 1, 1, S_T, FH),
            got("s_state", 1, 1, GH, GK, GV))
```
